# Optimizing a Trainium2 kernel written in Bass

```python
import math
import jax, jax.numpy as jnp
from jax import lax
import numpy as np

D_MODEL = 1024
BATCH = 1
SEQ = 512
DEPTH = 1
DEC_BATCH = 1
DEC_SEQ = 32
PAST_LEN = 512

CHUNK = 64
D_LRU = 1024
LRU_BLOCKS = 16
LRU_BW = D_LRU // LRU_BLOCKS
LRU_C = 8.0
CONV_W = 4
M_HEADS = 4
M_HD = 256
D_M = M_HEADS * M_HD
CONV_CH = D_LRU + 2 * D_M
IN_COLS = CONV_CH + 2 * D_M + 2 * M_HEADS + 2 * D_MODEL
N_GROUPS = 4
EXP_PER_GROUP = 4
N_EXPERTS = N_GROUPS * EXP_PER_GROUP
TOP_K_IN_GROUP = 2
D_EXPERT = 512
EPS = 1e-6

kernel_name = "hawk_mlstm_hmoe_streaming_step"

def _rmsnorm(x, g):
    x32 = x.astype(jnp.float32)
    y = x32 * lax.rsqrt(jnp.mean(x32 * x32, axis=-1, keepdims=True) + EPS)
    return (y * g.astype(jnp.float32)).astype(x.dtype)

def _causal_conv(u, prev, w, b):
    L = u.shape[1]
    full = jnp.concatenate([prev.astype(u.dtype), u], axis=1)
    out = full[:, 0:L] * w[0]
    for tap in range(1, CONV_W):
        out = out + full[:, tap:tap + L] * w[tap]
    return out + b, full[:, -(CONV_W - 1):]

def _rg_lru(x, h0, w_r, b_r, w_i, b_i, lam):
    Bn, L, _ = x.shape
    f32 = jnp.float32
    xb = x.reshape(Bn, L, LRU_BLOCKS, LRU_BW)
    r = jax.nn.sigmoid(jnp.einsum('blnc,ncd->blnd', xb, w_r).reshape(Bn, L, D_LRU) + b_r)
    i = jax.nn.sigmoid(jnp.einsum('blnc,ncd->blnd', xb, w_i).reshape(Bn, L, D_LRU) + b_i)
    log_a = -LRU_C * r.astype(f32) * jax.nn.softplus(-lam.astype(f32))
    a = jnp.exp(log_a)
    u = jnp.sqrt(-jnp.expm1(2.0 * log_a)) * (i * x).astype(f32)

    def comb(c1, c2):
        a1, b1 = c1
        a2, b2 = c2
        return a1 * a2, a2 * b1 + b2

    a_cum, b_cum = lax.associative_scan(comb, (a, u), axis=1)
    h = b_cum + a_cum * h0.astype(f32)[:, None]
    return h.astype(x.dtype), h[:, -1]

def _block_len(L):
    if L <= CHUNK:
        return L
    return CHUNK if L % CHUNK == 0 else math.gcd(L, CHUNK)

def _mlstm(q, k, v, i_pre, f_pre, C0, n0, m0):
    Bn, L, H, Dh = q.shape
    T = _block_len(L)
    NC = L // T
    f32 = jnp.float32

    def vec_chunks(a):
        return a.astype(f32).reshape(Bn, NC, T, H, Dh).transpose(1, 0, 3, 2, 4)

    def gate_chunks(a):
        return a.astype(f32).reshape(Bn, NC, T, H).transpose(1, 0, 3, 2)

    qc = vec_chunks(q)
    kc = vec_chunks(k) * (Dh ** -0.5)
    vc = vec_chunks(v)
    ic = gate_chunks(i_pre)
    lfc = gate_chunks(jax.nn.log_sigmoid(f_pre.astype(f32)))
    tri = jnp.tril(jnp.ones((T, T), dtype=bool))

    def step(carry, inp):
        C, n, m = carry
        qb, kb, vb, ib, lf = inp
        b = jnp.cumsum(lf, axis=-1)
        dlog = b[..., :, None] - b[..., None, :] + ib[..., None, :]
        dlog = jnp.where(tri, dlog, -jnp.inf)
        m_inter = b + m[..., None]
        m_t = jnp.maximum(m_inter, jnp.max(dlog, axis=-1))
        s = jnp.einsum('bhtd,bhsd->bhts', qb, kb) * jnp.exp(dlog - m_t[..., None])
        inter = jnp.exp(m_inter - m_t)
        num = jnp.einsum('bhts,bhsd->bhtd', s, vb) + inter[..., None] * jnp.einsum('bhvk,bhtk->bhtv', C, qb)
        den = jnp.sum(s, axis=-1) + inter * jnp.einsum('bhk,bhtk->bht', n, qb)
        h = num / jnp.maximum(jnp.abs(den), jnp.exp(-m_t))[..., None]
        bT = b[..., -1]
        m_new = m_t[..., -1]
        wk = jnp.exp(bT[..., None] - b + ib - m_new[..., None])
        decay = jnp.exp(bT + m - m_new)
        C_new = decay[..., None, None] * C + jnp.einsum('bhtv,bhtk->bhvk', vb * wk[..., None], kb)
        n_new = decay[..., None] * n + jnp.einsum('bht,bhtk->bhk', wk, kb)
        return (C_new, n_new, m_new), h

    (C, n, m), hs = lax.scan(step, (C0.astype(f32), n0.astype(f32), m0.astype(f32)),
                             (qc, kc, vc, ic, lfc))
    h = hs.transpose(1, 0, 3, 2, 4).reshape(Bn, L, H, Dh)
    return h, C, n, m

def _hmoe(x, w_group, b_group, w_erouter, b_erouter, w_gate, w_up, w_down):
    Bn, L, D = x.shape
    t = x.reshape(-1, D)
    f32 = jnp.float32
    gl = (t @ w_group + b_group).astype(f32)
    gp = jax.nn.softmax(gl, axis=-1)
    _, g_idx = lax.top_k(gl, 1)
    p_g = jnp.take_along_axis(gp, g_idx, axis=-1)
    el = (jnp.einsum('nd,gde->nge', t, w_erouter) + b_erouter).astype(f32)
    el_sel = jnp.take_along_axis(el, g_idx[:, :, None], axis=1)[:, 0]
    top_v, top_i = lax.top_k(el_sel, TOP_K_IN_GROUP)
    w2 = jax.nn.softmax(top_v, axis=-1) * p_g
    expert_id = g_idx * EXP_PER_GROUP + top_i
    combine = jnp.sum(jax.nn.one_hot(expert_id, N_EXPERTS, dtype=f32) * w2[..., None], axis=1)
    combine = combine.astype(x.dtype)
    out = jnp.zeros_like(t)
    for e in range(N_EXPERTS):
        hid = jax.nn.silu(t @ w_gate[e]) * (t @ w_up[e])
        out = out + combine[:, e:e + 1] * (hid @ w_down[e])
    return out.reshape(Bn, L, D)

def _layer(x, conv_prev, h0, C0, n0, m0, p):
    (g_mix, w_in, b_igate, b_fgate, conv_w, conv_b, lru_wr, lru_br, lru_wi, lru_bi, lru_lambda,
     m_gn, w_pa, w_pb, w_out, g_ffn, w_group, b_group, w_erouter, b_erouter,
     w_gate, w_up, w_down) = p
    Bn, L, _ = x.shape
    xn = _rmsnorm(x, g_mix)
    z = xn @ w_in
    c0 = CONV_CH
    v = z[..., c0:c0 + D_M]
    o = z[..., c0 + D_M:c0 + 2 * D_M]
    off = c0 + 2 * D_M
    i_pre = z[..., off:off + M_HEADS] + b_igate
    f_pre = z[..., off + M_HEADS:off + 2 * M_HEADS] + b_fgate
    off2 = off + 2 * M_HEADS
    g_a = z[..., off2:off2 + D_MODEL]
    g_b = z[..., off2 + D_MODEL:]
    conv_out, conv_state = _causal_conv(z[..., :c0], conv_prev, conv_w, conv_b)
    lru_y, h_last = _rg_lru(conv_out[..., :D_LRU], h0, lru_wr, lru_br, lru_wi, lru_bi, lru_lambda)
    qk = jax.nn.silu(conv_out[..., D_LRU:])
    q = qk[..., :D_M].reshape(Bn, L, M_HEADS, M_HD)
    k = qk[..., D_M:].reshape(Bn, L, M_HEADS, M_HD)
    hm, C, n, m = _mlstm(q, k, v.reshape(Bn, L, M_HEADS, M_HD), i_pre, f_pre, C0, n0, m0)
    hm = hm * lax.rsqrt(jnp.mean(hm * hm, axis=-1, keepdims=True) + EPS)
    m_y = (hm.reshape(Bn, L, D_M) * m_gn.astype(jnp.float32)).astype(x.dtype) * jax.nn.sigmoid(o)
    merged = jax.nn.sigmoid(g_a) * (lru_y @ w_pa) + jax.nn.sigmoid(g_b) * (m_y @ w_pb)
    x = x + merged @ w_out
    x = x + _hmoe(_rmsnorm(x, g_ffn), w_group, b_group, w_erouter, b_erouter, w_gate, w_up, w_down)
    dt = x.dtype
    return x, (conv_state.astype(dt), h_last.astype(dt), C.astype(dt), n.astype(dt), m.astype(dt))

def _trunk(x, conv0, h00, C00, n00, m00, params, g_final):
    convs, hs, Cs, ns, ms = [], [], [], [], []
    for l in range(DEPTH):
        p = [a[l] for a in params]
        x, (cs, hl, C, n, m) = _layer(x, conv0[l], h00[l], C00[l], n00[l], m00[l], p)
        convs.append(cs); hs.append(hl); Cs.append(C); ns.append(n); ms.append(m)
    y = _rmsnorm(x, g_final)
    return y, jnp.stack(convs), jnp.stack(hs), jnp.stack(Cs), jnp.stack(ns), jnp.stack(ms)

def setup_inputs(seed: int = 0) -> dict:
    key = jax.random.key(seed)
    ks = jax.random.split(key, 40)
    f32 = jnp.float32

    def nrm(k, shape, scale):
        return jax.random.normal(k, shape, f32) * scale

    u = jax.random.uniform(ks[15], (DEPTH, D_LRU), f32, 0.9, 0.999)
    s = u ** (1.0 / LRU_C)
    lru_lambda = jnp.log(s) - jnp.log1p(-s)
    return {
        "x_prompt": nrm(ks[0], (BATCH, SEQ, D_MODEL), 1.0),
        "x_sample": nrm(ks[1], (DEC_BATCH, DEC_SEQ, D_MODEL), 1.0),
        "state_conv": nrm(ks[2], (DEPTH, DEC_BATCH, CONV_W - 1, CONV_CH), 1.0),
        "state_lru": nrm(ks[3], (DEPTH, DEC_BATCH, D_LRU), 0.5),
        "state_mlstm_C": nrm(ks[4], (DEPTH, DEC_BATCH, M_HEADS, M_HD, M_HD), 0.05),
        "state_mlstm_n": jnp.abs(nrm(ks[5], (DEPTH, DEC_BATCH, M_HEADS, M_HD), 0.1)),
        "state_mlstm_m": nrm(ks[6], (DEPTH, DEC_BATCH, M_HEADS), 0.5),
        "g_mix": 1.0 + nrm(ks[7], (DEPTH, D_MODEL), 0.02),
        "w_in": nrm(ks[8], (DEPTH, D_MODEL, IN_COLS), D_MODEL ** -0.5),
        "b_igate": nrm(ks[9], (DEPTH, M_HEADS), 0.1),
        "b_fgate": jnp.linspace(3.0, 6.0, M_HEADS, dtype=f32)[None] + nrm(ks[10], (DEPTH, M_HEADS), 0.1),
        "conv_w": nrm(ks[11], (DEPTH, CONV_W, CONV_CH), CONV_W ** -0.5),
        "conv_b": nrm(ks[12], (DEPTH, CONV_CH), 0.01),
        "lru_wr": nrm(ks[13], (DEPTH, LRU_BLOCKS, LRU_BW, LRU_BW), LRU_BW ** -0.5),
        "lru_br": nrm(ks[14], (DEPTH, D_LRU), 0.01),
        "lru_wi": nrm(ks[16], (DEPTH, LRU_BLOCKS, LRU_BW, LRU_BW), LRU_BW ** -0.5),
        "lru_bi": nrm(ks[17], (DEPTH, D_LRU), 0.01),
        "lru_lambda": lru_lambda,
        "m_gn": 1.0 + nrm(ks[18], (DEPTH, D_M), 0.02),
        "w_pa": nrm(ks[19], (DEPTH, D_LRU, D_MODEL), D_LRU ** -0.5),
        "w_pb": nrm(ks[20], (DEPTH, D_M, D_MODEL), D_M ** -0.5),
        "w_out": nrm(ks[21], (DEPTH, D_MODEL, D_MODEL), D_MODEL ** -0.5),
        "g_ffn": 1.0 + nrm(ks[22], (DEPTH, D_MODEL), 0.02),
        "w_group": nrm(ks[23], (DEPTH, D_MODEL, N_GROUPS), D_MODEL ** -0.5),
        "b_group": nrm(ks[24], (DEPTH, N_GROUPS), 0.01),
        "w_erouter": nrm(ks[25], (DEPTH, N_GROUPS, D_MODEL, EXP_PER_GROUP), D_MODEL ** -0.5),
        "b_erouter": nrm(ks[26], (DEPTH, N_GROUPS, EXP_PER_GROUP), 0.01),
        "w_gate": nrm(ks[27], (DEPTH, N_EXPERTS, D_MODEL, D_EXPERT), D_MODEL ** -0.5),
        "w_up": nrm(ks[28], (DEPTH, N_EXPERTS, D_MODEL, D_EXPERT), D_MODEL ** -0.5),
        "w_down": nrm(ks[29], (DEPTH, N_EXPERTS, D_EXPERT, D_MODEL), D_EXPERT ** -0.5),
        "g_final": 1.0 + nrm(ks[30], (D_MODEL,), 0.02),
    }

def reference(x_prompt, x_sample, state_conv, state_lru, state_mlstm_C, state_mlstm_n, state_mlstm_m,
              g_mix, w_in, b_igate, b_fgate, conv_w, conv_b, lru_wr, lru_br, lru_wi, lru_bi, lru_lambda,
              m_gn, w_pa, w_pb, w_out, g_ffn, w_group, b_group, w_erouter, b_erouter,
              w_gate, w_up, w_down, g_final):
    params = (g_mix, w_in, b_igate, b_fgate, conv_w, conv_b, lru_wr, lru_br, lru_wi, lru_bi, lru_lambda,
              m_gn, w_pa, w_pb, w_out, g_ffn, w_group, b_group, w_erouter, b_erouter,
              w_gate, w_up, w_down)
    dt = x_prompt.dtype
    Bp = x_prompt.shape[0]
    zc = jnp.zeros((DEPTH, Bp, CONV_W - 1, CONV_CH), dt)
    zh = jnp.zeros((DEPTH, Bp, D_LRU), dt)
    zC = jnp.zeros((DEPTH, Bp, M_HEADS, M_HD, M_HD), dt)
    zn = jnp.zeros((DEPTH, Bp, M_HEADS, M_HD), dt)
    zm = jnp.zeros((DEPTH, Bp, M_HEADS), dt)
    y_prompt, p_conv, p_lru, p_C, p_n, p_m = _trunk(x_prompt, zc, zh, zC, zn, zm, params, g_final)
    y_sample, s_conv, s_lru, s_C, s_n, s_m = _trunk(x_sample, state_conv, state_lru, state_mlstm_C,
                                                    state_mlstm_n, state_mlstm_m, params, g_final)
    return (y_prompt, y_sample, p_conv, p_lru, p_C, p_n, p_m, s_conv, s_lru, s_C, s_n, s_m)


_drawn_inputs = setup_inputs


def setup_inputs(seed=0):
    import zlib

    import numpy as np

    out = dict(_drawn_inputs(seed))
    spreads = {}
    factors = {'lru_br': 21.959,
     'lru_bi': 8.0,
     'm_gn': 15.573,
     'b_group': 21.807,
     'b_erouter': 37.21,
     'g_final': 7.529,
     'g_ffn': 4.177}
    for name, (base, spread) in spreads.items():
        noise = np.random.default_rng([zlib.crc32(name.encode()), seed]).standard_normal(out[name].shape)
        drawn = base * np.exp(spread * noise) if base else spread * noise
        out[name] = __import__('jax').numpy.asarray(drawn.astype(out[name].dtype))
    for name, factor in factors.items():
        out[name] = (out[name] * factor).astype(out[name].dtype)
    return out
```

```python
from contextlib import ExitStack, contextmanager

import concourse.bass as bass
from concourse import mybir

P = 128
F32 = mybir.dt.float32
F32R = mybir.dt.float32r
BF16 = mybir.dt.bfloat16
I32 = mybir.dt.int32
U32 = mybir.dt.uint32
ALU = mybir.AluOpType
ACT = mybir.ActivationFunctionType
AX = mybir.AxisListType
ds = bass.ds


class Steps:

    def __init__(self, eng, sem):
        self.eng, self.sem, self.base, self.n = eng, sem, 0, 0

    def do(self, ins):
        self.n += 1
        ins.then_inc(self.sem, 1)

    def wait(self):
        self.eng.wait_ge(self.sem, self.base + self.n)

    def link(self, ins):
        self.do(ins)
        self.wait()

    @contextmanager
    def loop(self, count, per, start=0):
        base = self.base + self.n
        with self.eng.Fori(start, start + count) as i:
            self.base, self.n = i * per + (base - start * per), 0
            yield i
        assert self.n == per, f"{self.n} steps in the body, not {per}"
        self.base, self.n = base + count * per, 0


def hawk_mlstm_hmoe_kernel(
    nc, x_prompt, x_sample, state_conv, state_lru, state_mlstm_C, state_mlstm_n, state_mlstm_m,
    g_mix, w_in, b_igate, b_fgate, conv_w, conv_b, lru_wr, lru_br, lru_wi, lru_bi, lru_lambda,
    m_gn, w_pa, w_pb, w_out, g_ffn, w_group, b_group, w_erouter, b_erouter, w_gate, w_up, w_down, g_final,
    y_prompt, y_sample, p_conv, p_lru, p_C, p_n, p_m, s_conv, s_lru, s_C, s_n, s_m,
):
    D = x_prompt.shape[2]
    LP, LS = x_prompt.shape[1], x_sample.shape[1]
    N = LP + LS
    HB = N // 2
    KT = D // P
    JP = LP // P
    J = JP + 1
    H, HD = state_mlstm_C.shape[2], state_mlstm_C.shape[3]
    CT = HD // P
    CONV = conv_w.shape[2]
    NCT = CONV // P
    TAPS = conv_w.shape[1]
    PAD = TAPS - 1
    LN_ = LP + PAD + LS + 1
    S0 = LP + PAD
    CIN = LN_ + PAD
    NG, EG = w_erouter.shape[1], w_erouter.shape[3]
    NE, F = w_gate.shape[1], w_gate.shape[3]
    FT = F // P
    NR = NG + NG * EG
    EXTRA = (2 * N) // P
    TILES = NE + EXTRA
    TAB = TILES + 2
    EPS = 1e-6
    LRU_C = 8.0
    assert HB * 2 == N and HB <= 512 and CT == 2 and EG == NG

    win = w_in[0].rearrange("(k p) n -> p k n", p=P)
    wpa = w_pa[0].rearrange("(k p) n -> p k n", p=P)
    wpb = w_pb[0].rearrange("(k p) n -> p k n", p=P)
    wout = w_out[0].rearrange("(k p) n -> p k n", p=P)
    C_Q, C_K = D, D + H * HD
    C_V = CONV
    C_O = CONV + H * HD
    C_I = CONV + 2 * H * HD
    C_F = C_I + H
    C_A = C_F + H
    C_B = C_A + D
    GROUPS = [C_Q, C_Q + P, C_K, C_K + P, 0, P, C_V, C_V + P, C_O, C_O + P]
    NGR = len(GROUPS)
    RS = NGR // 2
    PJ_A0, PJ_BC, PJ_B0, PJ_LOOP, PJ_HEAD = 2, 6, 16, 26, 14
    PART_B = (4, 5, 6, 7, 10, 11)
    MS_HEAD, MS_PRE = 16, 12
    MC = KT // 2

    with ExitStack() as ctx:
        def sem(name):
            return ctx.enter_context(nc.semaphore(name))

        def dram(name, shape, dt):
            return nc.dram_tensor(name, shape, dt, kind="Internal").ap()

        t_dram = dram("t_rows", [N, D], F32)
        y_dram = dram("expert_rows", [TILES * P, D], F32)

        size = [0]
        cuts = {}

        def cut(name, n):
            cuts[name] = size[0]
            size[0] += -(-n // 8) * 8

        for name, n in (
            ("xh", KT * N), ("xl", KT * N), ("xpad", P - LS), ("w", RS * 2 * KT * P),
            ("lru", KT * N), ("my", KT * N), ("mb", H * N), ("en", H * N),
            ("q", CT * LN_), ("k", CT * LN_), ("xc", CT * LN_), ("cin", 2 * CIN), ("tmp", 4 * LN_),
            ("dp", 5 * 512), ("v", J * HD), ("kw", J * HD), ("c0", CT * HD), ("c0t", CT * HD),
            ("cout", 2 * CT * HD), ("nout", 2 * HD), ("og", CT * N), ("rs", 2 * N), ("qs", CT * LS),
            ("in", H * LS), ("n0rep", CT * P), ("n0row", HD),
            ("ident", P), ("ones", P), ("tri", P), ("sel", H * P), ("v1", P), ("v2", P), ("v1t", P), ("v2t", P),
            ("bd", CT * 2 * P), ("cols", J * 2 * H), ("cstate", 2 * PAD * NCT), ("lst", 2 * KT),
            ("small", 96), ("sig", 2 * N), ("counts", NE + EXTRA + 2 + P),
        ):
            cut(name, n)
        base = -(-nc.sbuf_base // 32) * 32
        rounded = ctx.enter_context(nc.sbuf_tensor("MEM_R", [P, size[0]], F32R))
        plain = nc.alloc_sbuf_tensor_at("MEM", [P, size[0]], F32, offset=base)

        def source(tensor, name, *dims, plus=0):
            n = 1
            for d in dims:
                n *= d
            v = nc.alloc_sbuf_tensor_at(tensor, [P, n], F32, offset=base + 4 * (cuts[name] + plus))[:, :]
            return v if len(dims) == 1 else v.rearrange("p (a b) -> p a b", a=dims[0])

        def at(name, *dims, plus=0, mem=plain):
            n = 1
            for d in dims:
                n *= d
            v = mem[:, cuts[name] + plus:cuts[name] + plus + n]
            if len(dims) == 1:
                return v
            if len(dims) == 2:
                return v.rearrange("p (a b) -> p a b", a=dims[0])
            return v.rearrange("p (a b c) -> p a b c", a=dims[0], b=dims[1])

        def parts(name, *dims, plus=0):
            n = 1
            for d in dims:
                n *= d
            return at(name, *dims, plus=plus, mem=rounded), at(name, *dims, plus=plus + n, mem=rounded)

        hl = [parts("w", KT, P, plus=s * 2 * KT * P) for s in range(RS)]
        raw = [source(f"RAW{s}", "w", KT, P, plus=(2 * s + 1) * KT * P) for s in range(RS)]
        w_slots = at("w", 2 * RS, KT, P, mem=rounded)
        hl_values = [w_slots[:, 2 + a:6 + a:2] for a in range(2)]
        xh, xl = parts("xh", KT, N)
        xflat = [at("xh", KT * N + P - LS, plus=m * KT * N, mem=rounded) for m in range(2)]
        lru_y, m_y = source("LRU_Y", "lru", KT, N), source("M_Y", "my", KT, N)
        Mb, En = at("mb", H, N), at("en", H, N)
        Inter = at("in", H, LS)
        q, k, xc = at("q", CT, LN_), at("k", CT, LN_), at("xc", CT, LN_)
        cin = at("cin", 2, CIN)
        tmp = at("tmp", 4, LN_)
        ri = tmp[:, 0:2, :], at("kw", 2, LN_)
        hh = at("tmp", CT, N)
        sq = at("tmp", CT, N, plus=CT * N)
        dp = at("dp", J, 512)
        v, kw = at("v", J, HD), at("kw", J, HD)
        c0, c0t = at("c0", CT, HD), at("c0t", CT, HD)
        cout = at("cout", 2, CT, HD)
        nout = at("nout", 2, HD)
        og = at("og", CT, N)
        rs = at("rs", 2, N)
        qs = at("qs", CT, LS)
        n0rep = at("n0rep", CT, P)
        n0row = at("n0row", HD)[0:1]
        out_rows = at("sel", 3, P)
        ident, ones, tri = at("ident", P), at("ones", P), at("tri", P)
        sel = at("sel", H, P)
        v1, v2, v1t, v2t = at("v1", P), at("v2", P), at("v1t", P), at("v2t", P)
        bd = at("bd", CT, 2, P)
        gcol = at("cols", J, 2 * H)
        cstate = at("cstate", 2, PAD, NCT)
        lst = at("lst", 2, KT)
        x_in = at("lru", J, D)
        xnb = at("q", 2, D)
        xt = source("XT", "dp", 4, 4 * P)
        bsig = xc
        row = {n: at("tmp", N, plus=m * N)[0:H] for m, n in enumerate(["f", "i", "lf", "b"])}
        row |= {n: at("og", N, plus=m * N)[0:H] for m, n in enumerate(["g", "M"])}
        row |= {n: at("v", N, plus=m * N)[0:H] for m, n in enumerate(["mt", "t1"])}
        row |= {n: at("rs", N, plus=m * N)[0:H] for m, n in enumerate(["wk", "ex"])}
        inter_row = at("nout", LS)[0:H]
        mout = at("small", 2, plus=0)[0:H]
        b_i, b_f, m0 = (at("small", 1, plus=2 + m)[0:H] for m in range(3))
        eps = at("small", 1, plus=6)
        ssq = at("small", J, plus=8)
        rstd = at("small", J, plus=14)
        newt = at("small", J, plus=48)
        cl = at("small", KT, plus=20)
        ltmp = at("small", KT, plus=28)
        neg_last = at("small", 2, plus=36)[0:H]
        x_junk = at("en", D)
        zeros = at("my", D, plus=(KT - 2) * N)

        V1C = {"cw": 0, "cb": TAPS * NCT, "lam": TAPS * NCT + NCT}
        V2C, at2 = {}, 0
        for n, c in (("br", KT), ("bi", KT), ("gn", KT), ("gmix", KT), ("h0", KT), ("n0", KT), ("sc", PAD * NCT)):
            V2C[n] = at2
            at2 += c
        V2R = at2

        branch = parts("mb", KT, N), parts("mb", KT, N, plus=2 * KT * N)
        halves = slice(0, KT // 2), slice(KT // 2, KT)
        merged_p = parts("lru", KT, N)
        late0 = 4 * KT * N - 2 * H * N
        sig2 = [at("sig", N, plus=m * N) for m in range(2)]
        mrg_in = [source(f"MERGED{m}", "q", N, plus=late0 + m * N) for m in range(2)]
        assert cuts["q"] + late0 + 2 * N <= cuts["ident"]
        x2 = at("xh", J, D)
        gffn = at("xh", D, plus=J * D)
        gfin = at("xh", D, plus=J * D + D)
        wr = at("xh", KT, NR, plus=J * D + 2 * D)
        brt = at("xh", NR, plus=J * D + 2 * D + KT * NR)
        CH = MC * F
        chunk_at = [cuts["mb"] + m * 2 * CH for m in range(2)] + [cuts["w"] + m * 2 * CH for m in range(4)]
        assert chunk_at[5] + 2 * CH <= chunk_at[0]
        chunk_dims = [(MC, F)] * 4 + [(FT // 2, D)] * 2
        moe_hl = [parts("w", *dims, plus=a - cuts["w"]) for a, dims in zip(chunk_at, chunk_dims)]
        moe_flat = [source(f"CHUNK{c}", "w", CH, plus=chunk_at[c] - cuts["w"] + CH) for c in range(6)]
        moe_raw = [flat.rearrange("p (k n) -> p k n", k=dims[0]) for flat, dims in zip(moe_flat, chunk_dims)]
        early_flat = [source(f"EARLY{m}", "q", CH, plus=chunk_at[1] + 2 * CH - cuts["q"] + J * D + 2 * D + 2 * N + m * CH) for m in range(2)]
        moe_early = [flat.rearrange("p (k n) -> p k n", k=MC) for flat in early_flat]
        moe_hl += [parts("w", FT // 2, D, plus=a - cuts["w"]) for a in chunk_at[:2]]
        moe_raw += [flat.rearrange("p (k n) -> p k n", k=FT // 2) for flat in moe_flat[:2]]
        at0 = chunk_at[1] + 2 * CH - cuts["q"]

        def late(plus, *dims, mem=plain):
            return at("q", *dims, plus=at0 + plus, mem=mem)

        assert cuts["q"] + at0 + 7680 <= cuts["ident"]
        T = late(0, J, D)
        tT = late(J * D, 2, D)
        yT = late(J * D + 2 * D, 2, N)
        assert cuts["q"] + at0 + J * D + 2 * D + 2 * N <= cuts["q"] + late0
        o = [J * D + 2 * D + KT * NR + NR]

        def small(*dims):
            n = 1
            for d in dims:
                n *= d
            got = at("xh", *dims, plus=o[0])
            o[0] += n
            assert o[0] <= cuts["w"] - cuts["xh"], o[0]
            return got

        lg, chosen = small(J, NR), small(J, NG, EG)
        gmax, gidx, pg, v1st, v2nd, i1, i2, w1, w2, dv = (small(J) for _ in range(10))
        t4, oh, io4, es = small(J, NG), small(J, NG), small(J, NG), small(J, NG)
        io16 = small(J, NE)
        A1, A2, AA, cum, tp = small(J, NE), small(J, NE), small(J, NE), small(J, NE), small(J, NE)
        before = small(J + 1, NE)
        ne, ext, xex, xin = small(NE), small(NE), small(NE), small(NE)
        e1, e2, r1, r2, x1, x2c, qn, qn2, tl1, tl2, ta, ta2 = (small(J) for _ in range(12))
        tp2, ssqp = small(J, NE), small(J, D // P)
        valid = small(J)
        tot = small(1)
        ioe = small(EXTRA)
        cmp8 = small(EXTRA, NE)
        te = small(TAB)
        tok_in, tok_first = small(J), small(J)
        io_tab, io_rank = at("counts", TAB), at("counts", P, plus=TAB)
        half_words = nc.alloc_sbuf_tensor_at("AT", [P, 2 * J * P + 4 * J * TAB], BF16, offset=base + 4 * (cuts["q"] + at0))
        at_rank = [half_words[:, m * J * P:(m + 1) * J * P].rearrange("p (j n) -> p j n", j=J) for m in range(2)]
        at_tile = [[half_words[:, 2 * J * P + (2 * m + n) * J * TAB:2 * J * P + (2 * m + n + 1) * J * TAB]
                    .rearrange("p (j n) -> p j n", j=J) for n in range(2)] for m in range(2)]
        is_tile = [late(J * P + 2 * J * TAB + m * J * TAB, J, TAB) for m in range(2)]
        slot_i = [small(J).bitcast(U32) for _ in range(2)]
        te_i = small(TAB).bitcast(I32)
        last_i = small(1).bitcast(I32)
        ids = small(TAB).bitcast(U32)
        xg = late(0, D)
        xgT = late(D, KT, P, mem=rounded), late(2 * D, KT, P, mem=rounded)
        sg, gs, hid = (late(3 * D + m * F, F) for m in range(3))
        hidT = tuple(late(3 * D + (3 + m) * F, FT, P, mem=rounded) for m in range(2))
        yt = late(3 * D + 5 * F, D)
        idcur = late(4 * D + 5 * F, 2).bitcast(U32)
        assert 4 * D + 5 * F + 2 <= 7680
        ya, yb = at("w", J, D), at("w", J, D, plus=J * D)
        fin = T

        PJ = ctx.enter_context(nc.psum_tensor("PJ", [P, 4, 512], F32))
        MS = ctx.enter_context(nc.psum_tensor("MS", [P, 2, 512], F32))
        NM = ctx.enter_context(nc.psum_tensor("NM", [P, 2, 512], F32))

        vec_in, small_in, consts = sem("vec_in"), sem("small_in"), sem("consts")
        x_in_landed = [sem(f"x_in_landed{j}") for j in range(J)]
        raw_in = [sem(f"raw_in{n}") for n in range(RS)]
        hi_done, lo_done = sem("hi_done"), sem("lo_done")
        c0_in, bd_in, head_out = sem("c0_in"), sem("bd_in"), sem("head_out")
        small_out, rows_zeroed, waits_passed = sem("small_out"), sem("rows_zeroed"), sem("waits_passed")
        ms_full, ms_free, pj_full, pj_free = sem("ms_full"), sem("ms_free"), sem("pj_full"), sem("pj_free")
        nm_full, nm_free = sem("nm_full"), sem("nm_free")
        steps_v, steps_a, steps_p = sem("steps_v"), sem("steps_a"), sem("steps_p")
        x_root, x_rstd, xnb_ready, xty, xh_ready, x_split = sem("x_root"), sem("x_rstd"), sem("xnb_ready"), sem("xty"), sem("xh_ready"), sem("x_split")
        lam_log, f_log, cl_ready = sem("lam_log"), sem("f_log"), sem("cl_ready")
        rows_scanned, rows_ready = sem("rows_scanned"), sem("rows_ready")
        dist_ready, dexp_ready, masked = sem("dist_ready"), sem("dexp_ready"), sem("masked")
        conv_done, sig_ready, silu_done = sem("conv_done"), sem("sig_ready"), sem("silu_done")
        decay_ready, poly_ready, root_ready, lru_done = sem("decay_ready"), sem("poly_ready"), sem("root_ready"), sem("lru_done")
        sq_ready, rms_root, my_done = sem("sq_ready"), sem("rms_root"), sem("my_done")
        branch_hi, last_states, rows_copied = sem("branch_hi"), sem("last_states"), sem("rows_copied")
        branch_split = [sem(f"branch_split{m}") for m in range(2)]
        mix_full, sig_done, mul_done, merged_split = sem("mix_full"), sem("sig_done"), sem("mul_done"), sem("merged_split")
        y_evac, x2_added = sem("y_evac"), sem("x2_added")
        x2_in, late_in, late_consts = sem("x2_in"), sem("late_in"), sem("late_consts")
        x2_squares, x2_ms, x2_root = sem("x2_squares"), sem("x2_ms"), sem("x2_root")
        t_ready, t_out, tT_full, tT_ready = sem("t_ready"), sem("t_out"), sem("tT_full"), sem("tT_ready")
        logits_done, gaps_ready, routing_exps = sem("logits_done"), sem("gaps_ready"), sem("routing_exps")
        choices_ready, cum_done, places_ready, slots_done, route_ready = (
            sem(n) for n in ("choices_ready", "cum_done", "places_ready", "slots_done", "route_ready"))
        chunk_in, chunk_hi, chunk_lo, chunk_used = (
            [sem(f"chunk_{what}{c}") for c in range(8)] for what in ("in", "hi", "lo", "used"))
        xg_in, xT_full, xT_hi, xgT_ready = sem("xg_in"), sem("xT_full"), sem("xT_hi"), sem("xgT_ready")
        sg_ready, gs_ready, hid_ready, hT_full, hT_hi, hidT_ready = (
            sem(n) for n in ("sg_ready", "gs_ready", "hid_ready", "hT_full", "hT_hi", "hidT_ready"))
        y0_ready, y1_ready, y_out, moe_done = sem("y0_ready"), sem("y1_ready"), sem("y_out"), sem("moe_done")
        ya_in = [sem(f"ya_in{j}") for j in range(J)]
        sum_ready, sum_squares, fin_root, fin_rstd, fin_scaled, fin_out = (
            sem(n) for n in ("sum_ready", "sum_squares", "fin_root", "fin_rstd", "fin_scaled", "fin_out"))
        fin_ready = [sem(f"fin_ready{j}") for j in range(J)]

        rows_of = [P] * JP + [LS]
        CONSTS, LATE_CONSTS = [0], [0]
        NCONST, NLATE = 12, 15
        V_HEAD = 61
        FIN_P = 3
        NCT2 = D // P
        NPJ, NMS = PJ_LOOP + (H - 1) * PJ_HEAD, MS_PRE + H * MS_HEAD
        W_MIX = 2 + H * NGR
        W_OUT = W_MIX + 4 * NCT2
        THREE = ((0, 0), (1, 0), (0, 1))

        def tok(j):
            return slice(P * j, P * j + rows_of[j])

        def part_a(hd):
            return PJ_A0 if isinstance(hd, int) and hd == 0 else hd * PJ_HEAD + (PJ_LOOP - PJ_HEAD)

        def part_b(hd):
            return hd * PJ_HEAD + PJ_B0

        def use_of(hd, g):
            return part_a(hd) + g if g < 4 else part_b(hd) + PART_B[g - 4] - 4

        def group_used(hd, g):
            return use_of(hd, 7 if g == 6 else g) + 1

        def landed(hd, g):
            return hd * 32 + 16 * (g // RS + 1 + (g % RS >= RS - 2))

        def mix_landed(n, m):
            return n * 16 + 16 * (2 * H + 1 + (m == RS - 2))

        def await_step(eng, semaphore, value):
            eng.wait_ge(semaphore, value)
            eng.sem_inc(waits_passed, 1)

        def three_passes(pe, out, w, x, first, last):
            for n, (a, b) in enumerate(THREE):
                ins = pe.matmul(out, w(a), x(b), start=first and n == 0, stop=last and n == 2)
            return ins

        block = ctx.enter_context(nc.Block())

        @block.sync
        def _(sp):
            def group(cols, w_slot):
                sp.dma_start(raw[w_slot], win[:, :, cols]).then_inc(raw_in[w_slot], 16)

            for j in range(J):
                src = x_prompt[0, tok(j), :] if j < JP else x_sample[0]
                sp.dma_start(x_in[0:rows_of[j], j, :], src).then_inc(x_in_landed[j], 16)
            for dst, r0, src in (
                (v1, V1C["cw"], conv_w[0].rearrange("t (c p) -> (t c) p", p=P)),
                (v1, V1C["cb"], conv_b[0].rearrange("(c p) -> c p", p=P)),
                (v1, V1C["lam"], lru_lambda[0].rearrange("(c p) -> c p", p=P)),
                (v2, V2C["br"], lru_br[0].rearrange("(c p) -> c p", p=P)),
                (v2, V2C["bi"], lru_bi[0].rearrange("(c p) -> c p", p=P)),
                (v2, V2C["gn"], m_gn[0].rearrange("(c p) -> c p", p=P)),
                (v2, V2C["gmix"], g_mix[0].rearrange("(c p) -> c p", p=P)),
                (v2, V2C["h0"], state_lru[0, 0].rearrange("(c p) -> c p", p=P)),
                (v2, V2C["n0"], state_mlstm_n[0, 0].rearrange("h (c p) -> (h c) p", p=P)),
                (v2, V2C["sc"], state_conv[0, 0].rearrange("t (c p) -> (t c) p", p=P)),
            ):
                sp.dma_start(dst[r0:r0 + src.shape[0], :], src).then_inc(vec_in, 16)
            group(slice(C_F, C_F + P), RS - 2)
            group(slice(C_I, C_I + P), RS - 1)
            for dst, src in ((b_i, b_igate[0]), (b_f, b_fgate[0]), (m0, state_mlstm_m[0, 0])):
                sp.dma_start(dst, src.rearrange("(h a) -> h a", a=1)).then_inc(small_in, 16)

            def load_group(hd, g, wait=True):
                if wait:
                    await_step(sp, pj_full, group_used(hd, g - RS) if g >= RS else group_used(hd - 1, g - RS + NGR))
                group(ds(GROUPS[g] + hd * CT * P, P), g % RS)

            def load_gates(hd):
                for m, w in enumerate((lru_wr, lru_wi)):
                    for half in range(2):
                        blocks = w[0].rearrange("(h c f) p d -> h f p c d", c=CT, f=2)
                        side = slice(64 * half, 64 * half + 64)
                        sp.dma_start(bd[side, :, m, side], blocks[ds(hd, 1), half].rearrange("a p c d -> p (a c) d"))\
                            .then_inc(bd_in, 16)

            def load_state(hd):
                sp.dma_start(c0, state_mlstm_C[0, 0, ds(hd, 1)].rearrange("a (c p) k -> p (a c) k", p=P)).then_inc(c0_in, 16)
                sp.dma_start(n0row, state_mlstm_n[0, 0, ds(hd, 1)]).then_inc(c0_in, 16)

            def store_state(hd):
                await_step(sp, ms_free, hd * MS_HEAD + (MS_PRE + 2 + 14))
                for m, (dC, dn) in enumerate(((p_C, p_n), (s_C, s_n))):
                    sp.dma_start(dC[0, 0, ds(hd, 1)].rearrange("a (c p) k -> p (a c) k", p=P), cout[:, m]).then_inc(head_out, 16)
                    sp.dma_start(dn[0, 0, ds(hd, 1)], nout[0:1, m, :]).then_inc(head_out, 16)

            for g in range(RS - 2):
                load_group(0, g, wait=False)
            sp.wait_ge(consts, NCONST)
            load_gates(0)
            load_state(0)
            for m in range(NE, TILES):
                sp.dma_start(y_dram[m * P:(m + 1) * P, :], zeros).then_inc(rows_zeroed, 16)
            for g in range(RS - 2, RS):
                sp.wait_ge(pj_full, g - (RS - 2) + 1)
                load_group(0, g, wait=False)
            for g in range(RS, NGR):
                load_group(0, g)
            for g in range(RS - 2):
                load_group(1, g)

            def head_loads(hd, ahead):
                for g in range(RS - 2, NGR):
                    load_group(hd, g)
                    if g == RS - 1:
                        await_step(sp, pj_full, hd * PJ_HEAD + (PJ_B0 - PJ_HEAD + 10))
                        load_gates(hd)
                    if g == 7:
                        store_state(hd - 1)
                        load_state(hd)
                if ahead:
                    for g in range(RS - 2):
                        load_group(hd + 1, g)

            with sp.Fori(1, H - 1) as hd:
                head_loads(hd, True)
            head_loads(H - 1, False)

            def chunk(c, e, dst=None):
                w, half = (w_gate, w_up, w_down, w_down)[c // 2], c % 2
                k = w.shape[2] // P // 2
                src = w[0, ds(e, 1), half * k * P:(half + 1) * k * P, :].rearrange("a (k p) n -> p (a k) n", p=P)
                sp.dma_start(moe_raw[c] if dst is None else dst, src).then_inc(chunk_in[c], 16)

            mix_src = (win[:, :, C_A:C_A + D], win[:, :, C_B:C_B + D], wpa, wpb)

            def load_mix(n, m):
                sp.dma_start(raw[m], mix_src[m][:, :, ds(n * P, P)]).then_inc(raw_in[m], 16)

            for m in range(4):
                sp.wait_ge(pj_full, group_used(H - 1, RS + m))
                load_mix(0, m)
            sp.wait_ge(mix_full, 1)
            load_mix(1, 0)
            store_state(H - 1)

            def mix_loads(n):
                for m in (1, 2, 3):
                    await_step(sp, mix_full, n * 4 + (m - 3))
                    load_mix(n, m)

            with sp.Fori(1, NCT2 - 1) as n:
                mix_loads(n)
                await_step(sp, mix_full, n * 4 + 1)
                load_mix(n + 1, 0)
            mix_loads(NCT2 - 1)
            for c in range(NCT2):
                sp.wait_ge(mix_full, 4 * (NCT2 - 1) + c + 1)
                sp.dma_start(raw[c % 4], wout[:, :, c * P:(c + 1) * P]).then_inc(raw_in[c % 4], 16)
                if c == 1:
                    sp.dma_start(x2[:, 0:JP, :], x_prompt[0].rearrange("(j p) d -> p j d", p=P)).then_inc(x2_in, 16)
                    sp.dma_start(x2[0:LS, JP, :], x_sample[0]).then_inc(x2_in, 16)
                if c == 3:
                    for m in range(2):
                        chunk(m, 0)
            sp.dma_start(gffn, g_ffn[0].partition_broadcast(P)).then_inc(late_in, 16)
            sp.dma_start(gfin, g_final.partition_broadcast(P)).then_inc(late_in, 16)
            sp.dma_start(wr[:, :, 0:NG], w_group[0].rearrange("(k p) n -> p k n", p=P)).then_inc(late_in, 16)
            for g in range(NG):
                sp.dma_start(wr[:, :, NG + g * EG:NG + (g + 1) * EG],
                             w_erouter[0, g].rearrange("(k p) n -> p k n", p=P)).then_inc(late_in, 16)
            sp.dma_start(brt[:, 0:NG], b_group[0].partition_broadcast(P)).then_inc(late_in, 16)
            sp.dma_start(brt[:, NG:NR], b_erouter[0].rearrange("g e -> (g e)").partition_broadcast(P)).then_inc(late_in, 16)

            sp.wait_ge(mix_full, 4 * NCT2 + NCT2)
            for c in range(2, 6):
                chunk(c, 0)
            for c in range(2):
                sp.wait_ge(chunk_in[c], 16)
                chunk(c, 1, dst=moe_early[c])
            sp.wait_ge(route_ready, 1)
            last = sp.value_load(last_i[0:1, 0:1], min_val=NE - 1, max_val=TILES - 1)

            def next_step(i, first=0):
                e_next = sp.value_load(te_i[0:1, ds(i + 1, 1)], min_val=0, max_val=NE - 1)
                for c in range(first, 4):
                    await_step(sp, chunk_used[c], i + 1)
                    chunk(c, e_next)

            next_step(0, first=2)
            with sp.Fori(1, TILES) as i:
                with sp.If(i < last):
                    next_step(i)
                    e_now = sp.value_load(te_i[0:1, ds(i, 1)], min_val=0, max_val=NE - 1)
                    for c in (4, 5):
                        await_step(sp, chunk_used[c], i)
                        chunk(c, e_now)
            e_last = sp.value_load(te_i[0:1, ds(last, 1)], min_val=0, max_val=NE - 1)
            for c in (6, 7):
                await_step(sp, chunk_used[c - 6], last + 1)
                chunk(c, e_last)
            for j in range(J):
                sp.wait_ge(fin_ready[j], 1)
                dst = y_prompt[0, P * j:P * (j + 1), :] if j < JP else y_sample[0]
                sp.dma_start(dst, fin[0:rows_of[j], j, :]).then_inc(fin_out, 16)
            sp.wait_ge(fin_out, 16 * J)

        @block.gpsimd
        def _(pool):
            st = Steps(pool, steps_p)
            tt = pool.tensor_tensor

            def const(ins):
                CONSTS[0] += 1
                ins.then_inc(consts, 1)

            def then(ins):
                const(ins)
                pool.wait_ge(consts, CONSTS[0])

            const(pool.memset(ssq, 0.0))
            const(pool.memset(eps, EPS))
            const(pool.memset(ones, 1.0))
            then(pool.memset(ident, 0.0))
            const(pool.affine_select(out=ident, in_=ident, compare_op=ALU.not_equal, fill=1.0, base=0,
                                     pattern=[[-1, P]], channel_multiplier=1))
            const(pool.memset(zeros, 0.0))
            const(pool.memset(at("xpad", P - LS, mem=rounded).bitcast(F32), 0.0))
            const(pool.memset(cin, 0.0))
            const(pool.memset(bd, 0.0))
            then(pool.memset(sel, 1.0))
            const(pool.affine_select(out=tri, in_=ones, compare_op=ALU.is_gt, fill=0.0, base=0,
                                     pattern=[[1, P]], channel_multiplier=-1))
            const(pool.affine_select(out=sel, in_=sel, compare_op=ALU.is_equal, fill=0.0, base=0,
                                     pattern=[[1, H], [0, P]], channel_multiplier=-1))

            def low(w, slot):
                await_step(pool, hi_done, w + 1)
                hi, lo = hl[slot]
                tt(lo, raw[slot], hi.bitcast(F32), ALU.subtract).then_inc(lo_done, 1)

            def low_group(hd, g):
                low(hd * NGR + (2 + g), g % RS)

            def masks(hd):
                for j in range(J):
                    await_step(pool, dexp_ready, hd * J + (j + 1))
                    d = dp[:, j, P * j:P * j + P] if j < JP else dp[0:LS, j, 0:LS]
                    pool.affine_select(out=d, in_=d, compare_op=ALU.is_ge, fill=0.0, base=0,
                                       pattern=[[1, rows_of[j]]], channel_multiplier=-1).then_inc(masked, 1)

            low(0, RS - 2)
            low(1, RS - 1)
            for g in range(8):
                low_group(0, g)
            pool.wait_ge(rows_scanned, 1)
            for m, dst in enumerate((p_m, s_m)):
                pool.dma_start(dst[0, 0].rearrange("(h a) -> h a", a=1), mout[:, m:m + 1]).then_inc(small_out, 16)
            masks(0)
            for g in range(8, 13):
                low_group(0, g)
            with pool.Fori(1, H) as hd:
                for g in (3, 4, 5):
                    low_group(hd, g)
                masks(hd)
                for g in range(6, 13):
                    low_group(hd, g)
            low(W_MIX + 3, 3)
            for m, half in enumerate(halves):
                pool.wait_ge(branch_hi, 1 + m)
                tt(branch[0][1][:, half], lru_y[:, half], branch[0][0][:, half].bitcast(F32), ALU.subtract).then_inc(branch_split[0], 1)
            with pool.Fori(1, NCT2) as n:
                for m in range(4):
                    low(n * 4 + (W_MIX + m), m)
            for c in range(NCT2):
                low(W_OUT + c, c % 4)

            def late_const(ins):
                LATE_CONSTS[0] += 1
                ins.then_inc(late_consts, 1)

            def count(out, pattern, mult=0):
                late_const(pool.iota(out, pattern=pattern, base=0, channel_multiplier=mult, allow_small_or_imprecise_dtypes=True))

            pool.wait_ge(mix_full, 4 * NCT2)
            count(io4, [[0, J], [1, NG]])
            count(io16, [[0, J], [1, NE]])
            count(ioe, [[1, EXTRA]])
            count(te, [[1, TAB]])
            count(tok_in, [[0, J]], 1)
            count(tok_first, [[P, J]])
            count(io_tab, [[1, TAB]])
            count(io_rank, [[1, P]])
            late_const(pool.memset(lg, 0.0))
            late_const(pool.memset(before[:, 0, :], 0.0))
            late_const(pool.memset(ssq, 0.0))
            late_const(pool.memset(valid, 1.0))
            pool.wait_ge(late_consts, LATE_CONSTS[0])
            for x in (valid, tok_in, tok_first):
                late_const(pool.affine_select(out=x, in_=x, compare_op=ALU.is_ge, fill=0.0, base=N - 1,
                                              pattern=[[-P, J]], channel_multiplier=-1))
            pool.wait_ge(rows_copied, 3)
            conv_rows = PAD * NCT
            pool.dma_start(p_conv[0, 0].rearrange("t (c p) -> (t c) p", p=P), out_rows[0:conv_rows, 0, :]).then_inc(small_out, 16)
            pool.dma_start(s_conv[0, 0].rearrange("t (c p) -> (t c) p", p=P), out_rows[0:conv_rows, 1, :]).then_inc(small_out, 16)
            pool.dma_start(p_lru[0, 0].rearrange("(c p) -> c p", p=P), out_rows[0:KT, 2, :]).then_inc(small_out, 16)
            pool.dma_start(s_lru[0, 0].rearrange("(c p) -> c p", p=P), out_rows[KT:2 * KT, 2, :]).then_inc(small_out, 16)

            for j in range(J):
                pool.wait_ge(t_ready, j + 1)
                pool.dma_start(t_dram[tok(j), :], T[0:rows_of[j], j, :]).then_inc(t_out, 16)

            def low_chunk(c, i):
                if c < 6:
                    await_step(pool, chunk_hi[c], i + 1)
                else:
                    pool.wait_ge(chunk_hi[c], 1)
                landed_at = moe_early if c < 2 and isinstance(i, int) and i == 1 else moe_raw
                tt(moe_hl[c][1], landed_at[c], moe_hl[c][0].bitcast(F32), ALU.subtract).then_inc(chunk_lo[c], 1)

            def gather(col):
                pool.tensor_copy(idcur[:, 0:1], ids[:, ds(col, 1)]).then_inc(steps_p, 1)
                await_step(pool, steps_p, col + 1)
                pool.indirect_dma_start(out=xg, out_offset=None, in_=t_dram,
                                        in_offset=bass.IndirectOffsetOnAxis(ap=idcur[:, 0:1], axis=0)).then_inc(xg_in, 16)

            low_chunk(1, 0)
            low_chunk(4, 0)
            pool.wait_ge(route_ready, 1)
            pool.wait_ge(t_out, 16 * J)
            last = pool.value_load(last_i[0:1, 0:1], min_val=NE - 1, max_val=TILES - 1)
            gather(0)
            pool.wait_ge(xT_full, 1)
            gather(1)

            def stage(i):
                low_chunk(1, i + 1)
                await_step(pool, xT_full, i + 2)
                gather(i + 2)

            stage(0)
            with pool.Fori(1, TILES) as i:
                with pool.If(i < last):
                    stage(i)
                    low_chunk(4, i)
            low_chunk(6, None)
            pool.wait_ge(moe_done, 1)
            for j in range(J):
                n = rows_of[j]
                for m, dst in enumerate((ya, yb)):
                    pool.indirect_dma_start(out=dst[0:n, j, :], out_offset=None, in_=y_dram,
                                            in_offset=bass.IndirectOffsetOnAxis(ap=slot_i[m][0:n, j:j + 1], axis=0)).then_inc(ya_in[j], 16)
            for j in range(FIN_P):
                pool.wait_ge(fin_scaled, j + 1)
                tt(fin[:, j, :], fin[:, j, :], gfin, ALU.mult).then_inc(fin_ready[j], 1)
            pool.wait_ge(small_out, 16 * 6)

        @block.scalar
        def _(act):
            st = Steps(act, steps_a)
            act.wait_ge(consts, 2)
            for j in range(J):
                n = rows_of[j]
                act.wait_ge(x_in_landed[j], 16)
                st.link(act.activation(x_junk[0:n], x_in[0:n, j, :], ACT.Square, accum_out=ssq[0:n, j:j + 1]))
            act.activation(rstd, ssq, ACT.Sqrt, bias=eps, scale=1.0 / D).then_inc(x_root, 1)

            def normalise(j):
                n = rows_of[j]
                if j >= 2:
                    act.wait_ge(ms_full, 2 + 2 * (j - 1))
                act.activation(xnb[0:n, j % 2, :], x_in[0:n, j, :], ACT.Copy, scale=rstd[0:n, j:j + 1]).then_inc(xnb_ready, 1)

            def high(slot, arrived):
                act.wait_ge(raw_in[slot], arrived)
                act.copy(hl[slot][0], raw[slot]).then_inc(hi_done, 1)

            def high_group(hd, g):
                high(g % RS, landed(hd + g // NGR, g % NGR) if g >= NGR else landed(hd, g))

            act.wait_ge(consts, NCONST)
            high(RS - 2, 16)
            high(RS - 1, 16)
            act.wait_ge(x_rstd, 1)
            normalise(0)
            normalise(1)
            for j in range(J):
                n = rows_of[j]
                for half in range(2):
                    u = 2 * j + half
                    act.wait_ge(xty, u + 1)
                    act.copy(xh[:, 4 * half:4 * half + 4, tok(j)], xt[:, u % 4, :].rearrange("p (m n) -> p m n", m=4)[:, :, 0:n])\
                        .then_inc(xh_ready, 1)
                    if half == 0 and 0 < j < J - 1:
                        normalise(j + 1)
            lam = v1t[:, V1C["lam"]:V1C["lam"] + KT]
            act.wait_ge(ms_free, 2 + 1)
            st.link(act.activation(ltmp, lam, ACT.Abs))
            st.link(act.activation(ltmp, ltmp, ACT.Exp, scale=-1.0))
            act.activation(ltmp, ltmp, ACT.Ln, bias=ones[:, 0:1]).then_inc(lam_log, 1)
            act.wait_ge(small_in, 48)
            for u, (r, b) in enumerate((("f", b_f), ("i", b_i))):
                high_group(0, u)
                act.wait_ge(pj_full, u + 1)
                act.activation(row[r].rearrange("p (a n) -> p a n", a=2), PJ[0:H, 2 * u:2 * u + 2, 0:HB], ACT.Identity, bias=b)\
                    .then_inc(pj_free, 1)
                if u == 1:
                    high_group(0, 2)
                else:
                    act.wait_ge(pj_free, 2 + 1)
                    st.link(act.activation(row["lf"], row["f"], ACT.Abs))
                    st.link(act.activation(row["lf"], row["lf"], ACT.Exp, scale=-1.0))
                    act.activation(row["lf"], row["lf"], ACT.Ln, bias=ones[0:H, 0:1]).then_inc(f_log, 1)

            def bank(use):
                act.wait_ge(pj_full, use + 1)

            def emptied(ins):
                ins.then_inc(pj_free, 1)

            def pj(u):
                return PJ[:, 2 * (u % 2):2 * (u % 2) + 2, :]

            def to_conv(hd, t):
                if t < 4:
                    high_group(hd, t + 3)
                bank(use_of(hd, t))
                b = pj(t)
                act.wait_ge(conv_done, hd * 6 + (t + 1))
                c = cin[:, t % 2, :]
                act.copy(c[:, PAD:PAD + HB], b[:, 0, 0:HB])
                act.copy(c[:, PAD + HB:PAD + LP], b[:, 1, 0:LP - HB])
                emptied(act.copy(c[:, S0 + PAD:S0 + PAD + LS], b[:, 1, LP - HB:HB]))

            def sigmoid_qk(hd, s):
                act.wait_ge(conv_done, hd * 6 + (s + 3))
                act.wait_ge(silu_done, hd * 4 + (s + 1))
                act.activation(bsig[:, s % 2, :], (q, k)[s // 2][:, s % 2, :], ACT.Sigmoid).then_inc(sig_ready, 1)

            def weights_exp(hd):
                for j in range(J):
                    act.wait_ge(dist_ready, hd * J + (j + 1))
                    d = dp[:, j, P * j:LP] if j < JP else dp[0:LS, j, 0:LS]
                    act.activation(d, d, ACT.Exp, scale=-1.0).then_inc(dexp_ready, 1)

            def squares(hd):
                act.wait_ge(ms_free, hd * MS_HEAD + (MS_PRE + 2 + 11))
                act.activation(sq, hh, ACT.Square).then_inc(sq_ready, 1)

            def head_root(hd):
                act.wait_ge(ms_free, hd * MS_HEAD + (MS_PRE + 2 + 16))
                act.activation(rs[:, 0, 0:N], rs[:, 1, 0:N], ACT.Sqrt).then_inc(rms_root, 1)

            def second_part(hd):
                for t in (4, 5):
                    to_conv(hd, t)
                high_group(hd, 8)
                high_group(hd, 9)
                bank(use_of(hd, 6))
                emptied(act.copy(v[:, 0:JP, :].rearrange("p j n -> p (j n)"), pj(0).rearrange("p a n -> p (a n)")))
                bank(use_of(hd, 7))
                emptied(act.copy(v[0:LS, JP, :], pj(1)[0:LS, 0, 0:HD]))
                if isinstance(hd, int) and hd == 0:
                    act.wait_ge(silu_done, 6)
                else:
                    act.wait_ge(my_done, hd)
                act.wait_ge(cl_ready, 1)

                def gates(c):
                    for m, name in enumerate(("br", "bi")):
                        bank(part_b(hd) + 4 + 4 * c + m)
                        emptied(act.activation(ri[c][:, m, :].rearrange("p (a n) -> p a n", a=2), pj(m)[:, :, 0:LN_ // 2], ACT.Sigmoid,
                                               bias=v2t[:, ds(hd * CT + (V2C[name] + c), 1)]))

                def decay(c):
                    act.wait_ge(pj_free, part_b(hd) + (2 + 4 + 4 * c + 1))
                    if c:
                        act.wait_ge(lru_done, hd * CT + c)
                    scale = cl[:, ds(hd * CT + c, 1)]
                    act.activation(tmp[:, 2, :], ri[c][:, 0, :], ACT.Exp, scale=scale)
                    act.activation(tmp[:, 3, :], ri[c][:, 0, :], ACT.Tanh, scale=scale).then_inc(decay_ready, 1)

                def root(c):
                    act.wait_ge(poly_ready, hd * CT + (c + 1))
                    act.activation(tmp[:, 3, :], ri[c][:, 0, :], ACT.Sqrt, scale=-1.0).then_inc(root_ready, 1)

                gates(0)
                decay(0)
                high_group(hd, 10)
                root(0)
                for m in range(CT):
                    high_group(hd, 11 + m)
                    bank(part_b(hd) + 6 + m)
                    emptied(act.activation(og[:, m, :].rearrange("p (a n) -> p a n", a=2), pj(m)[:, :, 0:HB], ACT.Sigmoid))
                gates(1)
                decay(1)
                root(1)

            to_conv(0, 0)
            to_conv(0, 1)
            act.wait_ge(rows_scanned, 1)
            st.do(act.activation(row["wk"][:, 0:LP], row["g"][:, 0:LP], ACT.Exp, bias=neg_last[:, 0:1]))
            st.do(act.activation(row["wk"][:, LP:N], row["g"][:, LP:N], ACT.Exp, bias=neg_last[:, 1:2]))
            st.do(act.activation(row["ex"], row["mt"], ACT.Exp, scale=-1.0))
            act.activation(inter_row, row["M"][:, LP:N], ACT.Exp, bias=m0, scale=-1.0).then_inc(rows_ready, 1)
            sigmoid_qk(0, 0)
            to_conv(0, 2)
            sigmoid_qk(0, 1)
            to_conv(0, 3)
            high_group(0, 7)
            sigmoid_qk(0, 2)
            sigmoid_qk(0, 3)
            for m in range(PJ_B0 - PJ_BC):
                bank(PJ_BC + m)
                b = pj(m)
                if m < 2 * H:
                    dst = (Mb if m < H else En)[:, m % H, :].rearrange("p (a n) -> p a n", a=2)
                    emptied(act.copy(dst, b[:, :, 0:HB]))
                elif m == 2 * H:
                    emptied(act.copy(Inter, b[:, 0, 0:H * LS].rearrange("p (h s) -> p h s", h=H)))
                else:
                    act.copy(gcol[:, 0:JP, :], b[:, 0, 0:JP * 2 * H].rearrange("p (j h) -> p j h", j=JP))
                    emptied(act.copy(gcol[0:LS, JP, :], b[0:LS, 0, JP * 2 * H:J * 2 * H]))
            weights_exp(0)
            second_part(0)
            with act.Fori(1, H) as hd:
                to_conv(hd, 0)
                to_conv(hd, 1)
                sigmoid_qk(hd, 0)
                squares(hd - 1)
                to_conv(hd, 2)
                sigmoid_qk(hd, 1)
                weights_exp(hd)
                to_conv(hd, 3)
                high_group(hd, 7)
                sigmoid_qk(hd, 2)
                head_root(hd - 1)
                sigmoid_qk(hd, 3)
                act.wait_ge(rows_zeroed, 16 * EXTRA)
                second_part(hd)

            def high_mix(n, m):
                high(m % 4, mix_landed(n + m // 4, m % 4))

            def gate(n, m):
                high_mix(n, m + 3)
                act.wait_ge(mix_full, n * 4 + (m + 1))
                if not (isinstance(n, int) and n == 0):
                    act.wait_ge(mul_done, n * 2 + (m - 1))
                act.activation(sig2[m].rearrange("p (a n) -> p a n", a=2), pj(m)[:, :, 0:HB], ACT.Sigmoid).then_inc(sig_done, 1)

            for m in range(2):
                gate(0, m)
            squares(H - 1)
            act.wait_ge(lru_done, H * CT)
            for half in halves:
                act.copy(branch[0][0][:, half], lru_y[:, half]).then_inc(branch_hi, 1)
            head_root(H - 1)
            act.wait_ge(my_done, H)
            act.wait_ge(head_out, 64 * H + 64)
            for half in halves:
                act.copy(branch[1][0][:, half], m_y[:, half]).then_inc(branch_hi, 1)
            with act.Fori(1, NCT2) as n:
                for m in (2, 3):
                    high_mix(n - 1, m + 3)
                for m in range(2):
                    gate(n, m)
            for m in (1, 2):
                high(m, mix_landed(NCT2, m))
            for c in range(NCT2):
                if c + 3 < NCT2:
                    high((c + 3) % 4, mix_landed(NCT2 + (c + 3) // 4, (c + 3) % 4))
                act.wait_ge(mix_full, 4 * NCT2 + c + 1)
                if c >= 2:
                    act.wait_ge(x2_added, 2 * (c - 1))
                act.copy(yT[:, c % 2, :].rearrange("p (a n) -> p a n", a=2), pj(c)[:, :, 0:HB]).then_inc(y_evac, 1)
                if c:
                    for j in range(J):
                        n = rows_of[j]
                        if j in (0, JP):
                            act.wait_ge(x2_added, 2 * (c - 1) + (1 if j == 0 else 2))
                        act.activation(T[0:n, j, (c - 1) * P:c * P], x2[0:n, j, (c - 1) * P:c * P], ACT.Square,
                                       accum_out=ssqp[0:n, j, c - 1:c]).then_inc(x2_squares, 1)
            for j in range(J):
                n = rows_of[j]
                if j in (0, JP):
                    act.wait_ge(x2_added, 2 * NCT2 - (1 if j == 0 else 0))
                act.activation(T[0:n, j, D - P:D], x2[0:n, j, D - P:D], ACT.Square, accum_out=ssqp[0:n, j, NCT2 - 1:NCT2]).then_inc(x2_squares, 1)
            act.wait_ge(x2_ms, 1)
            act.activation(rstd, ssq, ACT.Sqrt, bias=eps, scale=1.0 / D).then_inc(x2_root, 1)

            def high_chunk(c, i):
                act.wait_ge(chunk_in[c], i * 16 + 16 if c < 6 else 16)
                early = c < 2 and isinstance(i, int) and i == 1
                if early:
                    act.wait_ge(chunk_used[c], 1)
                act.copy(moe_hl[c][0], (moe_early if early else moe_raw)[c]).then_inc(chunk_hi[c], 1)

            high_chunk(0, 0)
            high_chunk(1, 0)
            for j in range(J):
                n = rows_of[j]
                if j >= 2:
                    act.wait_ge(logits_done, j - 1)
                for half in range(2):
                    act.wait_ge(tT_full, 2 * j + half + 1)
                    act.copy(tT[:, j % 2, half * 512:half * 512 + 512].rearrange("p (m n) -> p m n", m=4)[:, :, 0:n],
                             (MS, PJ)[j % 2][:, half, :].rearrange("p (m n) -> p m n", m=4)[:, :, 0:n]).then_inc(tT_ready, 1)
            high_chunk(2, 0)
            high_chunk(3, 0)
            act.wait_ge(gaps_ready, 1)
            act.activation(t4, t4, ACT.Exp).then_inc(routing_exps, 1)
            act.activation(dv, dv, ACT.Exp).then_inc(routing_exps, 1)
            high_chunk(4, 0)
            high_chunk(5, 0)

            act.wait_ge(route_ready, 1)
            last = act.value_load(last_i[0:1, 0:1], min_val=NE - 1, max_val=TILES - 1)

            def turned_rows(n):
                act.wait_ge(xT_full, n)
                act.copy(xgT[0].rearrange("p k n -> p (k n)"), MS.rearrange("p a n -> p (a n)")).then_inc(xT_hi, 1)

            def result(i, used):
                act.wait_ge(used, i if used is chunk_used[5] else 1)
                await_step(act, y_out, i * 16)
                act.copy(yt[:, 0:512], PJ[:, 2, :]).then_inc(y0_ready, 1)
                act.wait_ge(y0_ready, i)
                act.wait_ge(y1_ready, i)
                act.dma_start(y_dram[ds(i * P - P, P), :], yt).then_inc(y_out, 16)

            def gate(i):
                act.wait_ge(chunk_used[1], i + 1)
                act.activation(sg, PJ[:, 0, :], ACT.Sigmoid).then_inc(sg_ready, 1)

            def next_step(i):
                high_chunk(0, i + 1)
                high_chunk(1, i + 1)
                turned_rows(i + 2)
                high_chunk(2, i + 1)
                high_chunk(3, i + 1)

            def turned_hidden(i):
                act.wait_ge(hT_full, i + 1)
                act.copy(hidT[0].rearrange("p f n -> p (f n)"), NM[:, 0, :]).then_inc(hT_hi, 1)

            act.sem_inc(y_out, 16)
            turned_rows(1)
            gate(0)
            next_step(0)
            turned_hidden(0)
            with act.Fori(1, TILES) as i:
                with act.If(i < last):
                    gate(i)
                    next_step(i)
                    result(i, chunk_used[5])
                    turned_hidden(i)
                    high_chunk(4, i)
                    high_chunk(5, i)
            gate(last)
            high_chunk(6, last)
            high_chunk(7, last)
            result(last, chunk_used[5])
            turned_hidden(last)
            result(last + 1, chunk_used[7])
            await_step(act, y_out, last * 16 + 32)
            act.sem_inc(moe_done, 1)
            for j in range(J):
                n = rows_of[j]
                act.wait_ge(sum_ready, j + 1)
                act.activation(ya[0:n, j, :], fin[0:n, j, :], ACT.Square, accum_out=ssq[0:n, j:j + 1]).then_inc(sum_squares, 1)
                act.wait_ge(sum_squares, j + 1)
                act.activation(rstd[0:n, j:j + 1], ssq[0:n, j:j + 1], ACT.Sqrt, bias=eps[0:n], scale=1.0 / D).then_inc(fin_root, 1)
                if 0 < j <= FIN_P:
                    act.wait_ge(fin_rstd, j)
                    act.activation(fin[:, j - 1, :], fin[:, j - 1, :], ACT.Copy, scale=rstd[:, j - 1:j]).then_inc(fin_scaled, 1)

        @block.tensor
        def _(pe):
            pe.wait_ge(consts, NCONST)
            pe.wait_ge(vec_in, 160)

            def ms_use(n, hd=None):
                pe.wait_ge(ms_free, n + 1 if hd is None else hd * MS_HEAD + (MS_PRE + n + 1))
                return MS[:, n % 2, :]

            def filled(ins):
                ins.then_inc(ms_full, 1)

            def pj(u):
                return PJ[:, 2 * (u % 2):2 * (u % 2) + 2, :]

            filled(pe.transpose(ms_use(0)[:, 0:P], v1, ident))
            filled(pe.transpose(ms_use(1)[:, 0:V2R], v2[0:V2R], ident[0:V2R, 0:V2R]))
            for j in range(J):
                n = rows_of[j]
                pe.wait_ge(xnb_ready, j + 1)
                for half in range(2):
                    b = ms_use(2 + 2 * j + half)
                    for m in range(4):
                        last = pe.transpose(b[:, P * m:P * m + n], xnb[0:n, j % 2, ds((4 * half + m) * P, P)], ident[0:n, 0:n])
                    filled(last)
            pe.wait_ge(x_split, 2 * J)

            def columns(b, slot, w, x, signal):
                pe.wait_ge(lo_done, w + 1)
                for half in range(2):
                    for kt in range(KT):
                        last = three_passes(pe, b[:, half, 0:HB], lambda a: hl[slot][a][:, kt, :],
                                            lambda a: x[a][:, kt, half * HB:(half + 1) * HB], kt == 0, kt == KT - 1)
                last.then_inc(signal, 1)

            def project(hd, g):
                u = use_of(hd, g)
                pe.wait_ge(pj_free, u + 1)
                b = pj(g)
                columns(b, g % RS, hd * NGR + (2 + g), (xh, xl), pj_full)

            def values(hd):
                pe.wait_ge(lo_done, hd * NGR + (2 + 7 + 1))
                pe.wait_ge(pj_free, use_of(hd, 6) + 1)
                for j in range(J):
                    if j == JP:
                        pe.wait_ge(pj_free, use_of(hd, 7) + 1)
                    out = pj(j // JP)[:, (j % JP) // 2, (j % 2) * HD:(j % 2 + 1) * HD]
                    for kt in range(KT):
                        last = three_passes(pe, out, lambda a: xflat[a][:, kt * N + P * j:kt * N + P * (j + 1)],
                                            lambda a: hl_values[a][:, :, kt, :], kt == 0, kt == KT - 1)
                    if j >= JP - 1:
                        last.then_inc(pj_full, 1)

            for u in range(2):
                pe.wait_ge(pj_free, u + 1)
                columns(pj(u), RS - 2 + u, u, (xh, xl), pj_full)

            def second_part(hd):
                project(hd, 4)
                project(hd, 5)
                values(hd)
                await_step(pe, bd_in, hd * 64 + 64)
                for c in range(CT):
                    pe.wait_ge(conv_done, hd * 6 + (2 + 5 + c))
                    for m in range(2):
                        pe.wait_ge(pj_free, part_b(hd) + (4 + 4 * c + m + 1))
                        b = pj(m)
                        for half in range(2):
                            last = pe.matmul(b[:, half, 0:LN_ // 2], bd[:, c, m, :], xc[:, c, half * (LN_ // 2):(half + 1) * (LN_ // 2)],
                                             start=True, stop=True)
                        last.then_inc(pj_full, 1)
                    if c == 0:
                        project(hd, 8)
                        project(hd, 9)

            def keys_of(j):
                return slice(P * j, P * j + P) if j < JP else slice(S0, S0 + LS)

            def scores(hd):
                pe.wait_ge(c0_in, hd * 32 + 32)
                b = ms_use(0, hd)
                for kt in range(CT):
                    for vt in range(CT):
                        last = pe.transpose(b[:, kt * HD + vt * P:kt * HD + (vt + 1) * P], c0[:, vt, kt * P:(kt + 1) * P], ident)
                filled(last)
                pe.wait_ge(silu_done, hd * 4 + 6)
                for j in range(J):
                    b = ms_use(1 + j, hd)
                    quer = slice(P * j, LP) if j < JP else keys_of(j)
                    n = quer.stop - quer.start
                    for ct in range(CT):
                        last = pe.matmul(b[0:rows_of[j], 0:n], k[:, ct, keys_of(j)], q[:, ct, quer], start=ct == 0, stop=ct == CT - 1)
                    filled(last)
                for m in range(3):
                    b = ms_use(6 + m, hd)
                    for j in range(2 * m, min(2 * m + 2, J)):
                        for ct in range(CT):
                            last = pe.transpose(b[0:rows_of[j], (j % 2) * HD + ct * P:(j % 2) * HD + (ct + 1) * P], k[:, ct, keys_of(j)], ident)
                    filled(last)

            def numerators(hd):
                b = ms_use(9, hd)
                for j in range(JP):
                    last = pe.matmul(b[:, P * j:LP], ones, dp[:, j, P * j:LP], start=j == 0, stop=j == JP - 1)
                filled(last)
                pe.wait_ge(nm_free, hd + 1)
                for c in range(CT):
                    for j in range(JP):
                        last = pe.matmul(NM[:, c, P * j:LP], v[:, j, c * P:(c + 1) * P], dp[:, j, P * j:LP], start=j == 0, stop=j == JP - 1)
                last.then_inc(nm_full, 1)
                b = ms_use(10, hd)
                for c in range(CT + 1):
                    out = b[:, c * LS:(c + 1) * LS]
                    own = v[0:LS, JP, c * P:(c + 1) * P] if c < CT else ones[0:LS, :]
                    pe.matmul(out, own, dp[0:LS, JP, 0:LS], start=True, stop=False)
                    for kt in range(CT):
                        old = c0t[:, kt, c * P:(c + 1) * P] if c < CT else n0rep[:, kt, :]
                        last = pe.matmul(out, old, qs[:, kt, :], start=False, stop=kt == CT - 1)
                filled(last)

            def new_state(hd):
                for u, tiles in ((11, range(JP)), (12, [JP])):
                    b = ms_use(u, hd)
                    for c in range(CT):
                        for j in tiles:
                            n = rows_of[j]
                            last = pe.matmul(b[:, c * HD:(c + 1) * HD], v[0:n, j, c * P:(c + 1) * P], kw[0:n, j, :],
                                             start=j == tiles[0], stop=j == tiles[-1])
                    filled(last)
                b = ms_use(13, hd)
                for m, tiles in enumerate((range(JP), [JP])):
                    for j in tiles:
                        n = rows_of[j]
                        last = pe.matmul(b[:, m * HD:(m + 1) * HD], ones[0:n, :], kw[0:n, j, :], start=j == tiles[0], stop=j == tiles[-1])
                filled(last)

            def head_squares(hd):
                pe.wait_ge(sq_ready, hd + 1)
                for u, toks in ((14, slice(0, LP)), (15, slice(LP, N))):
                    b = ms_use(u, hd)
                    for c in range(CT):
                        last = pe.matmul(b[:, 0:toks.stop - toks.start], ones, sq[:, c, toks], start=c == 0, stop=c == CT - 1)
                    filled(last)

            for g in range(4):
                project(0, g)
            pe.wait_ge(rows_ready, 1)
            for m in range(PJ_B0 - PJ_BC):
                pe.wait_ge(pj_free, PJ_BC + m + 1)
                b = pj(m)
                if m < 2 * H:
                    src = row["M" if m < H else "ex"]
                    for half in range(2):
                        last = pe.matmul(b[:, half, 0:HB], sel[0:H, m % H, :], src[:, half * HB:(half + 1) * HB], start=True, stop=True)
                elif m == 2 * H:
                    for hd in range(H):
                        last = pe.matmul(b[:, 0, hd * LS:(hd + 1) * LS], sel[0:H, hd, :], inter_row, start=True, stop=True)
                else:
                    for j in range(J):
                        for s, src in enumerate((row["g"], row["wk"])):
                            last = pe.transpose(b[0:rows_of[j], 0, j * 2 * H + s * H:j * 2 * H + (s + 1) * H], src[:, tok(j)], ident[0:H, 0:H])
                last.then_inc(pj_full, 1)
            second_part(0)
            with pe.Fori(1, H) as hd:
                project(hd, 0)
                scores(hd - 1)
                project(hd, 1)
                numerators(hd - 1)
                project(hd, 2)
                new_state(hd - 1)
                project(hd, 3)
                head_squares(hd - 1)
                second_part(hd)

            def mix(n, m):
                operand = ((xh, xl), (xh, xl), *branch)[m]
                columns(pj(m), m, n * 4 + (W_MIX + m), operand, mix_full)

            scores(H - 1)
            pe.wait_ge(pj_free, NPJ + 2)
            mix(0, 0)
            numerators(H - 1)
            mix(0, 1)
            new_state(H - 1)
            head_squares(H - 1)

            def by_branch(n):
                for m in (2, 3):
                    pe.wait_ge(sig_done, n * 2 + (m - 1))
                    mix(n, m)

            def next_gates(n):
                for m in range(2):
                    pe.wait_ge(mul_done, n * 2 + (m + 1))
                    mix(n + 1, m)

            for m in (2, 3):
                pe.wait_ge(branch_split[m - 2], 2)
                pe.wait_ge(sig_done, m - 1)
                mix(0, m)
            pe.wait_ge(last_states, 1)
            b = ms_use(NMS)
            for m in range(2):
                pe.transpose(b[0:PAD * NCT, m * P:(m + 1) * P], cstate[:, m].rearrange("p t c -> p (t c)"), ident)
            filled(pe.transpose(b[0:2 * KT, 2 * P:3 * P], lst.rearrange("p t c -> p (t c)"), ident))
            next_gates(0)
            with pe.Fori(1, NCT2 - 1) as n:
                by_branch(n)
                next_gates(n)
            by_branch(NCT2 - 1)

            def turn_tile(c):
                pe.wait_ge(y_evac, c + 1)
                b = ms_use(NMS + 1 + 2 * c)
                for j in range(JP):
                    last = pe.transpose(b[:, P * j:P * (j + 1)], yT[:, c % 2, tok(j)], ident)
                filled(last)
                filled(pe.transpose(ms_use(NMS + 2 + 2 * c)[0:LS, 0:P], yT[:, c % 2, tok(JP)], ident))

            pe.wait_ge(merged_split, NCT2 + 1)
            for c in range(NCT2):
                if c < 2:
                    pe.wait_ge(mul_done, 2 * (NCT2 - 1) + c + 1)
                else:
                    pe.wait_ge(y_evac, c - 1)
                columns(pj(c), c % 4, W_OUT + c, merged_p, mix_full)
                if c:
                    turn_tile(c - 1)
            turn_tile(NCT2 - 1)
            pe.wait_ge(late_in, 16 * (5 + NG))
            pe.wait_ge(ms_free, NMS + 1 + 2 * NCT2 + 2)

            def logits(j):
                n = rows_of[j]
                pe.wait_ge(tT_ready, 2 * j + 2)
                for kt in range(KT):
                    last = pe.matmul(NM[0:n, 0, j * NR:(j + 1) * NR], tT[:, j % 2, kt * P:kt * P + n], wr[:, kt, :],
                                     start=kt == 0, stop=kt == KT - 1)
                last.then_inc(logits_done, 1)

            for j in range(J):
                n = rows_of[j]
                pe.wait_ge(t_ready, j + 1)
                for half in range(2):
                    if j >= 2:
                        pe.wait_ge(tT_ready, 2 * (j - 2) + half + 1)
                    b = (MS, PJ)[j % 2][:, half, :]
                    for m in range(4):
                        last = pe.transpose(b[:, P * m:P * m + n], T[0:n, j, (4 * half + m) * P:(4 * half + m + 1) * P], ident[0:n, 0:n])
                    last.then_inc(tT_full, 1)
                if j:
                    logits(j - 1)
            logits(J - 1)
            pe.wait_ge(choices_ready, 1)
            flat = before.rearrange("p j e -> p (j e)")
            pe.matmul(NM[:, 1, J * NE:(J + 1) * NE], ones, flat[:, J * NE:(J + 1) * NE], start=True, stop=True)
            pe.matmul(NM[:, 1, 0:J * NE], ones, flat[:, 0:J * NE], start=True, stop=False)
            pe.matmul(NM[:, 1, 0:J * NE], tri, AA.rearrange("p j e -> p (j e)"), start=False, stop=True).then_inc(cum_done, 1)
            pe.wait_ge(places_ready, 1)
            for m in range(2):
                for j in range(J):
                    for n in range(2):
                        last = pe.matmul(NM[:, 1, 128:128 + TAB], at_rank[m][:, j, :], at_tile[m][n][:, j, :],
                                         start=m + j + n == 0, stop=m == 1 and j == J - 1 and n == 1)
            last.then_inc(slots_done, 1)

            def turn_rows(n):
                await_step(pe, xg_in, n * 16)
                for half in range(2):
                    for m in range(4):
                        last = pe.transpose(MS[:, half, P * m:P * m + P], xg[:, (4 * half + m) * P:(4 * half + m + 1) * P], ident)
                last.then_inc(xT_full, 1)

            pe.wait_ge(route_ready, 1)
            turn_rows(1)
            last = pe.value_load(last_i[0:1, 0:1], min_val=NE - 1, max_val=TILES - 1)

            def gate_up(i):
                pe.wait_ge(xgT_ready, i + 1)
                for c in range(4):
                    pe.wait_ge(chunk_lo[c], i + 1)
                    for m in range(MC):
                        kt = (c % 2) * MC + m
                        last = three_passes(pe, PJ[:, c // 2, :], lambda a: xgT[a][:, kt, :], lambda a: moe_hl[c][a][:, m, :],
                                            kt == 0, kt == KT - 1)
                    last.then_inc(chunk_used[c], 1)

            def down(i, chunks=(4, 5)):
                pe.wait_ge(hidT_ready, i)
                for c in chunks:
                    pe.wait_ge(chunk_lo[c], i if c < 6 else 1)
                    for half in range(2):
                        for m in range(FT // 2):
                            f = (c % 2) * (FT // 2) + m
                            last = three_passes(pe, PJ[:, 2 + half, :], lambda a: hidT[a][:, f, :],
                                                lambda a: moe_hl[c][a][:, m, half * 512:(half + 1) * 512], f == 0, f == FT - 1)
                    last.then_inc(chunk_used[c], 1)

            def turn_hidden(i):
                pe.wait_ge(hid_ready, i + 1)
                for f in range(FT):
                    last = pe.transpose(NM[:, 0, f * P:(f + 1) * P], hid[:, f * P:(f + 1) * P], ident)
                last.then_inc(hT_full, 1)

            gate_up(0)
            turn_rows(2)
            turn_hidden(0)
            with pe.Fori(1, TILES) as i:
                with pe.If(i < last):
                    gate_up(i)
                    turn_rows(i + 2)
                    down(i)
                    turn_hidden(i)
            gate_up(last)
            down(last)
            turn_hidden(last)
            pe.wait_ge(y0_ready, last)
            pe.wait_ge(y1_ready, last)
            down(last + 1, chunks=(6, 7))

        @block.vector
        def _(dve):
            st = Steps(dve, steps_v)
            tt, ts, stt = dve.tensor_tensor, dve.tensor_scalar, dve.scalar_tensor_tensor
            dve.sem_inc(ms_free, 2)
            dve.sem_inc(pj_free, 2)
            dve.sem_inc(nm_free, 1)
            dve.sem_inc(conv_done, 2)
            dve.sem_inc(silu_done, 2)
            dve.sem_inc(head_out, 64)
            dve.sem_inc(merged_split, 1)
            dve.wait_ge(consts, NCONST)

            def emptied(ins):
                ins.then_inc(ms_free, 1)

            def refine(steps, rows, cols):
                r, s, m = rstd[rows, cols], newt[rows, cols], ssq[rows, cols]
                steps.link(dve.reciprocal(r, r))
                steps.link(ts(m, m, 1.0 / D, EPS, ALU.mult, ALU.add))
                steps.link(tt(s, r, r, ALU.mult))
                steps.link(tt(s, s, m, ALU.mult))
                steps.link(ts(s, s, -0.5, 1.5, ALU.mult, ALU.add))
                steps.link(tt(r, r, s, ALU.mult))

            dve.wait_ge(ms_full, 1)
            emptied(dve.tensor_copy(v1t, MS[:, 0, 0:P]))
            dve.wait_ge(ms_full, 2)
            emptied(dve.tensor_copy(v2t[:, 0:V2R], MS[:, 1, 0:V2R]))
            dve.wait_ge(x_root, 1)
            refine(st, slice(0, P), slice(0, J))
            dve.sem_inc(x_rstd, 1)

            gm = v2t[:, V2C["gmix"]:V2C["gmix"] + KT]
            dve.wait_ge(ms_free, 4)

            def rest_of_x(u):
                j, half = u // 2, u % 2
                n = rows_of[j]
                dve.wait_ge(xh_ready, u + 1)
                x = xt[:, u % 4, :].rearrange("p (m n) -> p m n", m=4)[:, :, 0:n]
                tt(xl[:, 4 * half:4 * half + 4, tok(j)], x, xh[:, 4 * half:4 * half + 4, tok(j)].bitcast(F32), ALU.subtract)\
                    .then_inc(x_split, 1)

            for j in range(J):
                n = rows_of[j]
                for half in range(2):
                    u = 2 * j + half
                    dve.wait_ge(ms_full, 2 + u + 1)
                    if u >= 4:
                        dve.wait_ge(x_split, u - 3)
                    x = xt[:, u % 4, :].rearrange("p (m n) -> p m n", m=4)[:, :, 0:n]
                    tt(x, MS[:, half, :].rearrange("p (m n) -> p m n", m=4)[:, :, 0:n],
                       gm[:, 4 * half:4 * half + 4].unsqueeze(2).to_broadcast([P, 4, n]), ALU.mult).then_inc(xty, 1)
                    dve.wait_ge(xty, u + 1)
                    dve.sem_inc(ms_free, 1)
                    if u:
                        rest_of_x(u - 1)
            rest_of_x(2 * J - 1)
            dve.wait_ge(lam_log, 1)
            st.link(stt(cl, v1t[:, V1C["lam"]:V1C["lam"] + KT], 0.0, ltmp, ALU.min, ALU.subtract))
            ts(cl, cl, LRU_C, None, ALU.mult).then_inc(cl_ready, 1)
            dve.wait_ge(f_log, 1)
            st.do(dve.memset(row["t1"], 1.0))
            st.link(stt(row["lf"], row["f"], 0.0, row["lf"], ALU.min, ALU.subtract))
            for s in (slice(0, LP), slice(LP, N)):
                st.do(dve.tensor_tensor_scan(row["b"][:, s], row["t1"][:, s], row["lf"][:, s], 0.0, ALU.mult, ALU.add))
            st.wait()
            dve.wait_ge(pj_free, 2 + 2)
            st.link(tt(row["g"], row["i"], row["b"], ALU.subtract))
            dve.wait_ge(small_in, 48)
            for s, start in ((slice(0, LP), 0.0), (slice(LP, N), m0)):
                st.do(dve.tensor_tensor_scan(row["M"][:, s], row["t1"][:, s], row["g"][:, s], start, ALU.mult, ALU.max))
            st.wait()
            st.link(tt(row["mt"], row["b"], row["M"], ALU.add))
            for m, t in enumerate((LP - 1, N - 1)):
                st.do(dve.tensor_copy(mout[:, m:m + 1], row["mt"][:, t:t + 1]))
                last = ts(neg_last[:, m:m + 1], row["M"][:, t:t + 1], -1.0, None, ALU.mult)
                st.do(last) if m == 0 else last.then_inc(rows_scanned, 1)

            def misc(hd, u):
                dve.wait_ge(ms_full, hd * MS_HEAD + (MS_PRE + u + 1))
                return MS[:, u % 2, :]

            def line(x):
                return x.rearrange("p a n -> p (a n)")

            def distances(hd):
                for j in range(J):
                    n = rows_of[j]
                    d, m = (dp[:, j, P * j:LP], slice(P * j, LP)) if j < JP else (dp[0:n, j, 0:LS], slice(LP, N))
                    ts(d, line(Mb[0:n, ds(hd, 1), m]), gcol[0:n, j, ds(hd, 1)], 0.0, ALU.subtract, ALU.max).then_inc(dist_ready, 1)
                for c in range(CT):
                    st.do(ts(n0rep[:, c, :], ones, v2t[:, ds(hd * CT + (V2C["n0"] + c), 1)], None, ALU.mult))

            def conv(hd, t):
                c = t % 2
                tile0 = (KT, 2 * KT, 0)[t // 2] + c
                dst = (q, k, xc)[t // 2][:, c, :]
                buf = cin[:, t % 2, :]
                dve.wait_ge(pj_free, use_of(hd, t) + 3)
                old = v2t[:, V2C["sc"]:V2C["sc"] + PAD * NCT].rearrange("p (t c) -> p t c", t=PAD)
                st.do(dve.tensor_copy(buf[:, S0:S0 + PAD].unsqueeze(2), old[:, :, ds(hd * CT + tile0, 1)]))
                for m, e in enumerate((PAD + LP, S0 + PAD + LS)):
                    st.do(dve.tensor_copy(cstate[:, m, :, ds(hd * CT + tile0, 1)], buf[:, e - PAD:e].unsqueeze(2)))
                st.wait()
                cw = [v1t[:, ds(hd * CT + (V1C["cw"] + tap * NCT + tile0), 1)] for tap in range(TAPS)]
                st.link(ts(dst, buf[:, 0:LN_], cw[0], v1t[:, ds(hd * CT + (V1C["cb"] + tile0), 1)], ALU.mult, ALU.add))
                for tap in range(1, TAPS):
                    ins = stt(dst, buf[:, tap:tap + LN_], cw[tap], dst, ALU.mult, ALU.add)
                    st.link(ins) if tap < TAPS - 1 else ins.then_inc(conv_done, 1)

            def silu(hd, s):
                dve.wait_ge(sig_ready, hd * 4 + (s + 1))
                x = (q, k)[s // 2][:, s % 2, :]
                if s < 2:
                    tt(x, x, bsig[:, s % 2, :], ALU.mult).then_inc(silu_done, 1)
                else:
                    stt(x, x, float(HD) ** -0.5, bsig[:, s % 2, :], ALU.mult, ALU.mult).then_inc(silu_done, 1)

            def lru(hd, c):
                r, u = ri[c][:, 0, :], ri[c][:, 1, :]
                dve.wait_ge(decay_ready, hd * CT + (c + 1))
                st.link(tt(r, tmp[:, 2, :], tmp[:, 2, :], ALU.mult))
                stt(r, r, 1.0, tmp[:, 3, :], ALU.add, ALU.mult).then_inc(poly_ready, 1)
                st.link(tt(u, u, xc[:, c, :], ALU.mult))
                dve.wait_ge(root_ready, hd * CT + (c + 1))
                st.link(tt(u, u, tmp[:, 3, :], ALU.mult))
                y = line(lru_y[:, ds(hd * CT + c, 1), :])
                st.do(dve.tensor_tensor_scan(y[:, 0:LP], tmp[:, 2, 0:LP], u[:, 0:LP], 0.0, ALU.mult, ALU.add))
                dve.tensor_tensor_scan(y[:, LP:N], tmp[:, 2, S0:S0 + LS], u[:, S0:S0 + LS],
                                       v2t[:, ds(hd * CT + (V2C["h0"] + c), 1)], ALU.mult, ALU.add).then_inc(lru_done, 1)

            def second_part(hd):
                dve.wait_ge(silu_done, hd * 4 + 6)
                for c in range(CT):
                    st.do(tt(qs[:, c, :], q[:, c, S0:S0 + LS], line(Inter[:, ds(hd, 1), :]), ALU.mult))
                conv(hd, 4)
                conv(hd, 5)
                lru(hd, 0)
                lru(hd, 1)

            def probabilities(hd):
                emptied(dve.tensor_copy(line(c0t), misc(hd, 0)))
                for j in range(J):
                    b = misc(hd, 1 + j)
                    dve.wait_ge(masked, hd * J + (j + 1))
                    d = dp[:, j, P * j:LP] if j < JP else dp[0:LS, j, 0:LS]
                    emptied(tt(d, b[0:d.shape[0], 0:d.shape[1]], d, ALU.mult))
                for j in range(J):
                    n = rows_of[j]
                    b = misc(hd, 6 + j // 2)
                    ins = ts(kw[0:n, j, :], b[0:n, (j % 2) * HD:(j % 2) * HD + HD], gcol[0:n, j, ds(hd + H, 1)], None, ALU.mult)
                    emptied(ins) if j % 2 or j == JP else st.do(ins)

            def head_results(hd):
                den, b = misc(hd, 9), misc(hd, 10)
                bound = line(En[:, ds(hd, 1), :])
                den_s = b[:, CT * LS:(CT + 1) * LS]
                st.do(stt(rs[:, 0, 0:LP], den, -1.0, bound[:, 0:LP], ALU.mult, ALU.max))
                st.link(stt(rs[:, 0, LP:N], den_s, -1.0, bound[:, LP:N], ALU.mult, ALU.max))
                emptied(tt(rs[:, 0, 0:LP], den, rs[:, 0, 0:LP], ALU.max))
                st.do(tt(rs[:, 0, LP:N], den_s, rs[:, 0, LP:N], ALU.max))
                dve.wait_ge(ms_free, hd * MS_HEAD + (MS_PRE + 2 + 10))
                st.wait()
                st.link(dve.reciprocal(rs[:, 0, :], rs[:, 0, :]))
                dve.wait_ge(nm_full, hd + 1)
                dve.wait_ge(lru_done, hd * CT + CT)
                st.do(tt(hh[:, 0, 0:LP], NM[:, 0, :], rs[:, 0, 0:LP], ALU.mult))
                tt(hh[:, 1, 0:LP], NM[:, 1, :], rs[:, 0, 0:LP], ALU.mult).then_inc(nm_free, 1)
                st.do(tt(hh[:, 0, LP:N], b[:, 0:LS], rs[:, 0, LP:N], ALU.mult))
                emptied(tt(hh[:, 1, LP:N], b[:, LS:2 * LS], rs[:, 0, LP:N], ALU.mult))

            def new_state(hd):
                decay = line(Inter[:, ds(hd, 1), LS - 1:LS])
                dve.wait_ge(head_out, hd * 64 + 64)
                emptied(dve.tensor_copy(line(cout[:, 0]), misc(hd, 11)))
                emptied(stt(line(cout[:, 1]), line(c0), decay, misc(hd, 12), ALU.mult, ALU.add))
                b = misc(hd, 13)
                st.do(dve.tensor_copy(nout[0:1, 0, :], b[0:1, 0:HD]))
                emptied(stt(nout[0:1, 1, :], n0row, decay[0:1], b[0:1, HD:2 * HD], ALU.mult, ALU.add))

            def mean_squares(hd):
                emptied(ts(rs[:, 1, 0:LP], misc(hd, 14), 1.0 / HD, EPS, ALU.mult, ALU.add))
                emptied(ts(rs[:, 1, LP:N], misc(hd, 15)[:, 0:LS], 1.0 / HD, EPS, ALU.mult, ALU.add))

            def branch_rows(hd):
                dve.wait_ge(rms_root, hd + 1)
                st.link(dve.reciprocal(rs[:, 1, :], rs[:, 0, :]))
                for c in range(CT):
                    st.do(stt(hh[:, c, :], hh[:, c, :], v2t[:, ds(hd * CT + (V2C["gn"] + c), 1)], rs[:, 1, :], ALU.mult, ALU.mult))
                st.wait()
                st.do(tt(line(m_y[:, ds(hd * CT, 1), :]), hh[:, 0, :], og[:, 0, :], ALU.mult))
                tt(line(m_y[:, ds(hd * CT + 1, 1), :]), hh[:, 1, :], og[:, 1, :], ALU.mult).then_inc(my_done, 1)

            conv(0, 0)
            conv(0, 1)
            silu(0, 0)
            conv(0, 2)
            silu(0, 1)
            conv(0, 3)
            silu(0, 2)
            silu(0, 3)
            dve.wait_ge(pj_free, PJ_B0 + 2)
            distances(0)
            second_part(0)
            with st.loop(H - 1, V_HEAD, start=1) as hd:
                probabilities(hd - 1)
                conv(hd, 0)
                head_results(hd - 1)
                silu(hd, 0)
                distances(hd)
                new_state(hd - 1)
                conv(hd, 1)
                conv(hd, 2)
                silu(hd, 1)
                mean_squares(hd - 1)
                conv(hd, 3)
                silu(hd, 2)
                branch_rows(hd - 1)
                silu(hd, 3)
                second_part(hd)
            probabilities(H - 1)
            head_results(H - 1)
            new_state(H - 1)
            mean_squares(H - 1)
            branch_rows(H - 1)
            dve.wait_ge(lru_done, H * CT)
            for m, t in enumerate((LP - 1, N - 1)):
                ins = dve.tensor_copy(lst[:, m, :], lru_y[:, :, t])
                st.do(ins) if m == 0 else ins.then_inc(last_states, 1)
            for m, half in enumerate(halves):
                dve.wait_ge(branch_hi, 3 + m)
                tt(branch[1][1][:, half], m_y[:, half], branch[1][0][:, half].bitcast(F32), ALU.subtract).then_inc(branch_split[1], 1)
            with st.loop(NCT2, 2) as n:
                dve.wait_ge(merged_split, n + 1)
                for m in range(2):
                    dve.wait_ge(mix_full, n * 4 + (m + 3))
                    dve.wait_ge(sig_done, n * 2 + (m + 1))
                    xv = sig2[m].rearrange("p (a n) -> p a n", a=2)
                    dst = mrg_in[m].rearrange("p (a n) -> p a n", a=2)
                    tt(dst, PJ[:, 2 * m:2 * m + 2, 0:HB], xv, ALU.mult).then_inc(mul_done, 1)
                dve.wait_ge(mul_done, n * 2 + 2)
                st.link(tt(mrg_in[0], mrg_in[0], mrg_in[1], ALU.add))
                st.link(dve.tensor_copy(line(merged_p[0][:, ds(n, 1), :]), mrg_in[0]))
                tt(line(merged_p[1][:, ds(n, 1), :]), mrg_in[0], line(merged_p[0][:, ds(n, 1), :]).bitcast(F32), ALU.subtract)\
                    .then_inc(merged_split, 1)
            dve.wait_ge(ms_full, NMS + 1)
            for m in range(3):
                n = PAD * NCT if m < 2 else 2 * KT
                dve.tensor_copy(out_rows[0:n, m, :], MS[0:n, NMS % 2, m * P:(m + 1) * P]).then_inc(rows_copied, 1)
            dve.wait_ge(rows_copied, 3)
            dve.sem_inc(ms_free, 1)
            dve.wait_ge(x2_in, 32)
            for c in range(NCT2):
                u = NMS + 1 + 2 * c
                dve.wait_ge(ms_full, u + 1)
                x = x2[:, 0:JP, c * P:(c + 1) * P]
                tt(x, MS[:, u % 2, :].rearrange("p (j n) -> p j n", j=JP), x, ALU.add).then_inc(x2_added, 1)
                dve.wait_ge(ms_full, u + 2)
                x = x2[0:LS, JP, c * P:(c + 1) * P]
                tt(x, MS[0:LS, (u + 1) % 2, 0:P], x, ALU.add).then_inc(x2_added, 1)
                dve.wait_ge(x2_added, 2 * c + 2)
                dve.sem_inc(ms_free, 2)
            dve.wait_ge(late_consts, NLATE)
            dve.wait_ge(late_in, 16 * (5 + NG))
            dve.wait_ge(x2_squares, J * NCT2)
            st.do(dve.tensor_reduce(ssq[:, 0:JP], ssqp[:, 0:JP, :], AX.X, ALU.add))
            dve.tensor_reduce(ssq[0:LS, JP:J], ssqp[0:LS, JP:J, :], AX.X, ALU.add).then_inc(x2_ms, 1)
            dve.wait_ge(x2_root, 1)
            refine(st, slice(0, P), slice(0, J))
            for j in range(J):
                n = rows_of[j]
                stt(T[0:n, j, :], x2[0:n, j, :], rstd[0:n, j:j + 1], gffn[0:n], ALU.mult, ALU.mult).then_inc(t_ready, 1)

            def low_chunk(c, i):
                dve.wait_ge(chunk_hi[c], i + 1 if c < 6 else 1)
                landed_at = moe_early if c < 2 and isinstance(i, int) and i == 1 else moe_raw
                tt(moe_hl[c][1], landed_at[c], moe_hl[c][0].bitcast(F32), ALU.subtract).then_inc(chunk_lo[c], 1)

            low_chunk(0, 0)
            dve.wait_ge(logits_done, J)
            for j in range(J):
                n = rows_of[j]
                st.do(tt(lg[0:n, j, :], NM[0:n, 0, j * NR:(j + 1) * NR], brt[0:n], ALU.add))
            st.wait()
            L = st.link

            def col(x):
                return x.unsqueeze(2)

            def spread(x, n):
                return col(x).to_broadcast([P, J, n])

            def first_max(x, best, onehot, index):
                L(dve.tensor_reduce(best, x, AX.X, ALU.max))
                L(tt(onehot, x, spread(best, NG), ALU.is_lt))
                L(stt(onehot, onehot, 64.0, io4, ALU.mult, ALU.add))
                L(dve.tensor_reduce(index, onehot, AX.X, ALU.min))
                L(tt(onehot, io4, spread(index, NG), ALU.is_equal))

            gl = lg[:, :, 0:NG]
            first_max(gl, gmax, oh, gidx)
            L(tt(t4, gl, spread(gmax, NG), ALU.subtract))
            eg = lg[:, :, NG:NR].rearrange("p j (g e) -> p j g e", g=NG)
            L(tt(chosen, eg, oh.unsqueeze(3).to_broadcast([P, J, NG, EG]), ALU.mult))
            L(dve.tensor_reduce(es, chosen.rearrange("p j g e -> p j e g"), AX.X, ALU.add))
            first_max(es, v1st, oh, i1)
            L(stt(es, oh, -3.0e38, es, ALU.mult, ALU.add))
            first_max(es, v2nd, oh, i2)
            tt(dv, v2nd, v1st, ALU.subtract).then_inc(gaps_ready, 1)
            for idx, e in ((i1, e1), (i2, e2)):
                L(stt(e, gidx, float(EG), idx, ALU.mult, ALU.add))
            for A, e in ((A1, e1), (A2, e2)):
                L(tt(A, io16, spread(e, NE), ALU.is_equal))
                L(tt(A, A, spread(valid, NE), ALU.mult))
            L(tt(AA, A1, A2, ALU.add))
            for j in range(J):
                ins = tt(before[:, j + 1, :], before[:, j, :], AA[:, j, :], ALU.add)
                L(ins) if j < J - 1 else ins.then_inc(choices_ready, 1)
            dve.wait_ge(cum_done, 1)
            st.do(dve.tensor_copy(cum, NM[:, 1, 0:J * NE].rearrange("p (j e) -> p j e", j=J)))
            L(dve.tensor_copy(ne, NM[:, 1, J * NE:(J + 1) * NE]))
            L(ts(ext, ne, float(P) + 0.5, None, ALU.is_gt))
            for m in range(2, J):
                L(stt(ext, ne, float(P * m) + 0.5, ext, ALU.is_gt, ALU.add))
            L(dve.tensor_tensor_scan(xin, ones[:, 0:NE], ext, 0.0, ALU.mult, ALU.add))
            st.do(ts(tot, xin[:, NE - 1:NE], float(NE - 1), None, ALU.add))
            L(tt(xex, xin, ext, ALU.subtract))
            st.do(dve.tensor_copy(last_i, tot))
            L(tt(cmp8, xin.unsqueeze(1).to_broadcast([P, EXTRA, NE]), ioe.unsqueeze(2).to_broadcast([P, EXTRA, NE]), ALU.is_le))
            L(dve.tensor_reduce(te[:, NE:TILES], cmp8, AX.X, ALU.add))
            L(ts(te, te, float(NE - 1), None, ALU.min))
            st.do(dve.tensor_copy(te_i, te))
            both = ((A1, e1, r1, x1, tl1, tp, qn, ta), (A2, e2, r2, x2c, tl2, tp2, qn2, ta2))

            def each(op):
                for one in both:
                    st.do(op(*one))
                st.wait()

            def spread_e(x):
                return x.unsqueeze(1).to_broadcast([P, J, NE])

            each(lambda A, e, r, x, tl, tp, qn, ta: tt(tp, A, cum, ALU.mult))
            each(lambda A, e, r, x, tl, tp, qn, ta: dve.tensor_reduce(r, tp, AX.X, ALU.add))
            each(lambda A, e, r, x, tl, tp, qn, ta: tt(tp, A, spread_e(xex), ALU.mult))
            each(lambda A, e, r, x, tl, tp, qn, ta: dve.tensor_reduce(x, tp, AX.X, ALU.add))
            each(lambda A, e, r, x, tl, tp, qn, ta: ts(qn, r, float(P) - 0.5, None, ALU.is_gt))
            for n in range(2, J):
                each(lambda A, e, r, x, tl, tp, qn, ta: stt(qn, r, float(P * n) - 0.5, qn, ALU.is_gt, ALU.add))
            each(lambda A, e, r, x, tl, tp, qn, ta: stt(r, qn, -float(P), r, ALU.mult, ALU.add))
            each(lambda A, e, r, x, tl, tp, qn, ta: ts(ta, qn, 0.5, None, ALU.is_gt))
            each(lambda A, e, r, x, tl, tp, qn, ta: stt(tl, x, float(NE - 1), qn, ALU.add, ALU.add))
            each(lambda A, e, r, x, tl, tp, qn, ta: tt(tl, tl, e, ALU.subtract))
            each(lambda A, e, r, x, tl, tp, qn, ta: tt(tl, tl, ta, ALU.mult))
            each(lambda A, e, r, x, tl, tp, qn, ta: tt(tl, tl, e, ALU.add))
            iot = io_tab.unsqueeze(1).to_broadcast([P, J, TAB])
            ior = io_rank.unsqueeze(1).to_broadcast([P, J, P])
            dve.wait_ge(t_out, 16 * J)
            for m, one in enumerate(both):
                st.do(tt(at_rank[m], ior, spread(one[2], P), ALU.is_equal))
                st.do(tt(is_tile[m], iot, spread(one[4], TAB), ALU.is_equal))
            st.wait()
            for m in range(2):
                st.do(tt(at_tile[m][0], is_tile[m], spread(tok_in, TAB), ALU.mult))
                last = tt(at_tile[m][1], is_tile[m], spread(tok_first, TAB), ALU.mult)
                st.do(last) if m == 0 else last.then_inc(places_ready, 1)
            each(lambda A, e, r, x, tl, tp, qn, ta: stt(ta, tl, float(P), r, ALU.mult, ALU.add))
            for m in range(2):
                st.do(dve.tensor_copy(slot_i[m], (ta, ta2)[m]))
            dve.wait_ge(slots_done, 1)
            L(dve.tensor_copy(ids, NM[:, 1, 128:128 + TAB]))
            dve.sem_inc(route_ready, 1)
            dve.wait_ge(routing_exps, 2)
            L(dve.tensor_reduce(pg, t4, AX.X, ALU.add))
            L(dve.reciprocal(pg, pg))
            L(ts(w1, dv, 1.0, None, ALU.add))
            L(dve.reciprocal(w1, w1))
            L(tt(w1, w1, pg, ALU.mult))
            st.do(tt(w2, w1, dv, ALU.mult))

            def rest_of_rows(n):
                dve.wait_ge(xT_hi, n)
                tt(line(xgT[1]), line(MS), line(xgT[0]).bitcast(F32), ALU.subtract).then_inc(xgT_ready, 1)

            def second_half(i, used):
                dve.wait_ge(used, i if used is chunk_used[5] else 1)
                await_step(dve, y_out, i * 16)
                dve.tensor_copy(yt[:, 512:1024], PJ[:, 3, :]).then_inc(y1_ready, 1)

            last = dve.value_load(last_i[0:1, 0:1], min_val=NE - 1, max_val=TILES - 1)

            def gate(i):
                dve.wait_ge(sg_ready, i + 1)
                tt(gs, PJ[:, 0, :], sg, ALU.mult).then_inc(gs_ready, 1)

            def hidden(i):
                dve.wait_ge(gs_ready, i + 1)
                dve.wait_ge(chunk_used[3], i + 1)
                tt(hid, PJ[:, 1, :], gs, ALU.mult).then_inc(hid_ready, 1)

            def rest_of_hidden(i):
                dve.wait_ge(hT_hi, i + 1)
                tt(line(hidT[1]), NM[:, 0, :], line(hidT[0]).bitcast(F32), ALU.subtract).then_inc(hidT_ready, 1)

            rest_of_rows(1)
            low_chunk(2, 0)
            low_chunk(3, 0)
            gate(0)
            low_chunk(0, 1)
            hidden(0)
            rest_of_rows(2)
            low_chunk(2, 1)
            low_chunk(3, 1)
            rest_of_hidden(0)
            low_chunk(5, 0)
            with dve.Fori(1, TILES) as i:
                with dve.If(i < last):
                    gate(i)
                    low_chunk(0, i + 1)
                    hidden(i)
                    rest_of_rows(i + 2)
                    low_chunk(2, i + 1)
                    low_chunk(3, i + 1)
                    second_half(i, chunk_used[5])
                    rest_of_hidden(i)
                    low_chunk(5, i)
            gate(last)
            hidden(last)
            low_chunk(7, last)
            second_half(last, chunk_used[5])
            rest_of_hidden(last)
            second_half(last + 1, chunk_used[7])
            fv = Steps(dve, sem("sum_steps"))

            def finish(j):
                n = rows_of[j]
                dve.wait_ge(fin_root, j + 1)
                refine(fv, slice(0, n), slice(j, j + 1))
                if j < FIN_P:
                    dve.sem_inc(fin_rstd, 1)
                else:
                    stt(fin[0:n, j, :], fin[0:n, j, :], rstd[0:n, j:j + 1], gfin[0:n], ALU.mult, ALU.mult).then_inc(fin_ready[j], 1)

            for j in range(J):
                n = rows_of[j]
                dve.wait_ge(ya_in[j], 32)
                fv.link(stt(fin[0:n, j, :], ya[0:n, j, :], w1[0:n, j:j + 1], x2[0:n, j, :], ALU.mult, ALU.add))
                stt(fin[0:n, j, :], yb[0:n, j, :], w2[0:n, j:j + 1], fin[0:n, j, :], ALU.mult, ALU.add).then_inc(sum_ready, 1)
                if j:
                    finish(j - 1)
            finish(J - 1)


_INS = ['x_prompt', 'x_sample', 'state_conv', 'state_lru', 'state_mlstm_C', 'state_mlstm_n', 'state_mlstm_m',
        'g_mix', 'w_in', 'b_igate', 'b_fgate', 'conv_w', 'conv_b', 'lru_wr', 'lru_br', 'lru_wi', 'lru_bi', 'lru_lambda',
        'm_gn', 'w_pa', 'w_pb', 'w_out', 'g_ffn', 'w_group', 'b_group', 'w_erouter', 'b_erouter',
        'w_gate', 'w_up', 'w_down', 'g_final']
_OUTS = [(1, 512, 1024), (1, 32, 1024), (1, 1, 3, 3072), (1, 1, 1024), (1, 1, 4, 256, 256), (1, 1, 4, 256), (1, 1, 4),
         (1, 1, 3, 3072), (1, 1, 1024), (1, 1, 4, 256, 256), (1, 1, 4, 256), (1, 1, 4)]


def kernel(**inputs):
    import numpy as _np
    import concourse.bacc as _bacc
    from concourse import mybir as _mybir
    from concourse.bass_utils import run_bass_kernel_spmd as _run

    nc = _bacc.Bacc("TRN2", target_bir_lowering=False, num_devices=1)
    arrays, args = {}, []
    for name in _INS:
        a = _np.ascontiguousarray(inputs[name])
        arrays[f"in_{name}_dram"] = a
        args.append(nc.dram_tensor(f"in_{name}_dram", a.shape, _mybir.dt.from_np(a.dtype), kind="ExternalInput").ap())
    for i, shape in enumerate(_OUTS):
        args.append(nc.dram_tensor(f"out_{i}_dram", shape, _mybir.dt.float32, kind="ExternalOutput").ap())
    hawk_mlstm_hmoe_kernel(nc, *args)
    r = _run(nc, [arrays], core_ids=[0])
    return tuple(r.results[0][f"out_{i}_dram"] for i in range(len(_OUTS)))
```
